# Optimizing a Trainium2 kernel written in Bass

```python
import math
import jax
import jax.numpy as jnp
from jax import lax
import numpy as np
import jax, jax.numpy as jnp

D_MODEL = 1024
BATCH = 1
SEQ = 256
DEPTH = 1

GRID_W = 64
CTX_LEN = 256
N_MIXERS = 4
D_FF = 4 * D_MODEL
N_MOD = 6
EPS = 1e-6
CONV_W = 3
HG_HEAD_DIM = 128
HG_HEADS = D_MODEL // HG_HEAD_DIM
HG_CHUNK = 32
S5_GROUP = 16
S5_GROUPS = D_MODEL // S5_GROUP
S5_STATE = 64
S5_DT_MIN = 1e-3
S5_DT_MAX = 1e-1
NA_HEADS = 16
NA_HEAD_DIM = D_MODEL // NA_HEADS
NA_ROWS = 8
NA_COLS = 16
NA_STRIP = 2 * NA_COLS


def _layers_of(mixer):
    return len(range(mixer, DEPTH, N_MIXERS))

def rmsnorm(x, g):
    xf = x.astype(jnp.float32)
    y = xf * lax.rsqrt(jnp.mean(xf * xf, axis=-1, keepdims=True) + EPS)
    return (y * g.astype(jnp.float32)).astype(x.dtype)

def modulate(h, shift, scale):
    return h * (1 + scale) + shift

def squared_relu_mlp(h, w_in, w_out):
    return jnp.square(jax.nn.relu(h @ w_in)) @ w_out

def depthwise_conv3(u, w):
    return lax.conv_general_dilated(u, w.astype(u.dtype)[:, None, :], window_strides=(1,),
                                    padding=((1, 1),), dimension_numbers=('NWC', 'WIO', 'NWC'),
                                    feature_group_count=u.shape[-1])

def short_gated_conv(h, w_in, conv_w, w_out):
    b_gate, c_gate, v = jnp.split(h @ w_in, 3, axis=-1)
    return (b_gate * depthwise_conv3(c_gate * v, conv_w)) @ w_out

def gla_chunked(q, k, v, log_f, s0):
    bsz, seq, nh, dk = q.shape
    dv = v.shape[-1]
    nc = seq // HG_CHUNK

    def chunks(t):
        return t.reshape(bsz, nc, HG_CHUNK, nh, t.shape[-1]).transpose(1, 0, 3, 2, 4)

    qc, kc, vc = chunks(q.astype(jnp.float32)), chunks(k.astype(jnp.float32)), chunks(v)
    b = jnp.cumsum(chunks(log_f.astype(jnp.float32)), axis=3)
    b_mid = b[:, :, :, HG_CHUNK // 2 - 1:HG_CHUNK // 2]
    b_last = b[:, :, :, -1:]
    scores = jnp.einsum('nbhtk,nbhsk->nbhts', qc * jnp.exp(b - b_mid), kc * jnp.exp(b_mid - b))
    prefix = jnp.tril(jnp.ones((HG_CHUNK, HG_CHUNK), dtype=bool))
    o_intra = jnp.einsum('nbhts,nbhsv->nbhtv', jnp.where(prefix, scores, 0.0), vc)
    q_out = qc * jnp.exp(b)
    k_state = kc * jnp.exp(b_last - b)
    decay_chunk = jnp.exp(b_last[:, :, :, 0, :])

    def step(s, xs):
        q_o, k_s, v_s, a = xs
        o = jnp.einsum('bhtk,bhkv->bhtv', q_o, s)
        s = a[..., None] * s + jnp.einsum('bhtk,bhtv->bhkv', k_s, v_s)
        return s, o

    s_fin, o_inter = lax.scan(step, s0, (q_out, k_state, vc, decay_chunk))
    o = (o_intra + o_inter).transpose(1, 0, 3, 2, 4).reshape(bsz, seq, nh, dv)
    return o, s_fin

def hgrn2_mixer(h_ctx, h_lat, w_in, lower_bound, g_norm, w_out, ctx_out):
    bsz = h_lat.shape[0]
    s0 = jnp.zeros((bsz, HG_HEADS, HG_HEAD_DIM, HG_HEAD_DIM), jnp.float32)

    def heads(t):
        return t.reshape(*t.shape[:2], HG_HEADS, HG_HEAD_DIM)

    def forget(t):
        f = lower_bound + (1 - lower_bound) * jax.nn.sigmoid(t.astype(jnp.float32))
        return heads(1 - f), heads(jnp.log(f))

    def project(h):
        q, inp, gate, f_fwd, f_bwd = jnp.split(h @ w_in, 5, axis=-1)
        return heads(q), heads(inp), gate, forget(f_fwd), forget(f_bwd)

    def flip(t):
        return t[:, ::-1]

    qc, vc, gc, (kcf, lcf), (kcb, lcb) = project(h_ctx)
    ql, vl, gl, (klf, llf), (klb, llb) = project(h_lat)
    oc_f, st_f = gla_chunked(qc, kcf, vc, lcf, s0)
    ol_f, _ = gla_chunked(ql, klf, vl, llf, st_f)
    oc_b, st_b = gla_chunked(flip(qc), flip(kcb), flip(vc), flip(lcb), s0)
    ol_b, _ = gla_chunked(flip(ql), flip(klb), flip(vl), flip(llb), st_b)

    def readout(o, gate):
        o = rmsnorm(o, g_norm.reshape(HG_HEADS, HG_HEAD_DIM))
        o = o.reshape(*o.shape[:2], D_MODEL).astype(gate.dtype)
        return (o * jax.nn.silu(gate)) @ w_out

    y_lat = readout(ol_f + flip(ol_b), gl)
    y_ctx = readout(oc_f + flip(oc_b), gc) if ctx_out else None
    return y_ctx, y_lat

def s5_discretise(lam_re, lam_im, log_dt, b_re, b_im):
    lam_re = jnp.minimum(lam_re.astype(jnp.float32), -1e-4)
    lam_im = lam_im.astype(jnp.float32)
    dt = jnp.exp(log_dt.astype(jnp.float32))[:, None]
    mag = jnp.exp(lam_re * dt)
    a_re, a_im = mag * jnp.cos(lam_im * dt), mag * jnp.sin(lam_im * dt)
    den = lam_re * lam_re + lam_im * lam_im
    f_re = ((a_re - 1) * lam_re + a_im * lam_im) / den
    f_im = (a_im * lam_re - (a_re - 1) * lam_im) / den
    b_re, b_im = b_re.astype(jnp.float32), b_im.astype(jnp.float32)
    bb_re = f_re[..., None] * b_re - f_im[..., None] * b_im
    bb_im = f_re[..., None] * b_im + f_im[..., None] * b_re
    return a_re, a_im, bb_re, bb_im

def s5_scan(bu_re, bu_im, a_re, a_im, init, reverse):
    if init is not None:
        i_re, i_im = init
        first = -1 if reverse else 0
        bu_re = bu_re.at[:, first].add(a_re * i_re - a_im * i_im)
        bu_im = bu_im.at[:, first].add(a_re * i_im + a_im * i_re)
    seq = bu_re.shape[1]
    a_seq_re = jnp.broadcast_to(a_re, (1, seq) + a_re.shape)
    a_seq_im = jnp.broadcast_to(a_im, (1, seq) + a_im.shape)

    def combine(e1, e2):
        a1r, a1i, b1r, b1i = e1
        a2r, a2i, b2r, b2i = e2
        return (a2r * a1r - a2i * a1i, a2r * a1i + a2i * a1r,
                a2r * b1r - a2i * b1i + b2r, a2r * b1i + a2i * b1r + b2i)

    _, _, x_re, x_im = lax.associative_scan(combine, (a_seq_re, a_seq_im, bu_re, bu_im),
                                            axis=1, reverse=reverse)
    return x_re, x_im

def s5_mixer(h_ctx, h_lat, lam_re, lam_im, log_dt, b_re, b_im, c_re, c_im, d_skip, w_glu, ctx_out):
    def grouped(h):
        return h.reshape(*h.shape[:2], S5_GROUPS, S5_GROUP).astype(jnp.float32)

    u_c, u_l = grouped(h_ctx), grouped(h_lat)
    d = d_skip.reshape(S5_GROUPS, S5_GROUP).astype(jnp.float32)
    y_c, y_l = d * u_c, d * u_l
    for direction in range(2):
        reverse = direction == 1
        a_re, a_im, bb_re, bb_im = s5_discretise(lam_re[direction], lam_im[direction],
                                                 log_dt[direction], b_re, b_im)
        cr, ci = c_re[direction].astype(jnp.float32), c_im[direction].astype(jnp.float32)

        def drive(u):
            return (jnp.einsum('bsgc,gnc->bsgn', u, bb_re), jnp.einsum('bsgc,gnc->bsgn', u, bb_im))

        def readout(xr, xi):
            return jnp.einsum('bsgn,gcn->bsgc', xr, cr) - jnp.einsum('bsgn,gcn->bsgc', xi, ci)

        xc_re, xc_im = s5_scan(*drive(u_c), a_re, a_im, None, reverse)
        end = 0 if reverse else -1
        xl_re, xl_im = s5_scan(*drive(u_l), a_re, a_im, (xc_re[:, end], xc_im[:, end]), reverse)
        y_l = y_l + readout(xl_re, xl_im)
        if ctx_out:
            y_c = y_c + readout(xc_re, xc_im)

    def glu(y):
        z = jax.nn.gelu(y.reshape(*y.shape[:2], D_MODEL)).astype(w_glu.dtype)
        val, gate = jnp.split(z @ w_glu, 2, axis=-1)
        return val * jax.nn.sigmoid(gate)

    return (glu(y_c) if ctx_out else None), glu(y_l)

def neighbourhood_attention(h_ctx, h_lat, w_qkv, rpb, w_out, ctx_out):
    bsz, seq, _ = h_lat.shape
    rows = seq // GRID_W
    kr = min(NA_ROWS, rows)
    n_cb = GRID_W // NA_COLS
    n_loc = kr * NA_STRIP
    scale = NA_HEAD_DIM ** -0.5

    def heads(t):
        return t.reshape(*t.shape[:2], NA_HEADS, NA_HEAD_DIM)

    q_l, k_l, v_l = (heads(t) for t in jnp.split(h_lat @ w_qkv, 3, axis=-1))
    k_c, v_c = (heads(t) for t in jnp.split(h_ctx @ w_qkv[:, D_MODEL:], 2, axis=-1))

    r = jnp.arange(rows)
    key_rows = jnp.clip(r - kr // 2, 0, rows - kr)[:, None] + jnp.arange(kr)
    qcol = (jnp.arange(n_cb) * NA_COLS)[:, None] + jnp.arange(NA_COLS)
    key_cols = (jnp.clip(jnp.arange(n_cb) * NA_COLS - NA_COLS // 2, 0, GRID_W - NA_STRIP)[:, None]
                + jnp.arange(NA_STRIP))
    q_start = jnp.clip(qcol - NA_COLS // 2, 0, GRID_W - NA_COLS)[..., None]
    kcol = key_cols[:, None, :]
    in_win = jnp.tile((kcol >= q_start) & (kcol < q_start + NA_COLS), (1, 1, kr))
    dr = key_rows - r[:, None] + (NA_ROWS - 1)
    dc = jnp.clip(kcol - qcol[..., None], 1 - NA_COLS, NA_COLS - 1) + (NA_COLS - 1)
    bias = rpb[:, dr[:, None, None, :, None], dc[None, :, :, None, :]]
    bias = bias.reshape(NA_HEADS, rows, n_cb, NA_COLS, n_loc).astype(jnp.float32)

    def gather(t):
        g = t.reshape(bsz, rows, GRID_W, NA_HEADS, NA_HEAD_DIM)
        g = g[:, key_rows[:, None, :, None], key_cols[None, :, None, :]]
        return g.reshape(bsz, rows, n_cb, n_loc, NA_HEADS, NA_HEAD_DIM)

    q_b = q_l.reshape(bsz, rows, n_cb, NA_COLS, NA_HEADS, NA_HEAD_DIM)
    k_win, v_win = gather(k_l), gather(v_l)
    s_loc = jnp.einsum('brjqhd,brjkhd->bhrjqk', q_b, k_win).astype(jnp.float32) * scale + bias
    s_loc = jnp.where(in_win, s_loc, -jnp.inf)
    s_ctx = jnp.einsum('brjqhd,bkhd->bhrjqk', q_b, k_c).astype(jnp.float32) * scale
    p = jax.nn.softmax(jnp.concatenate([s_loc, s_ctx], axis=-1), axis=-1).astype(v_l.dtype)
    o = (jnp.einsum('bhrjqk,brjkhd->brjqhd', p[..., :n_loc], v_win)
         + jnp.einsum('bhrjqk,bkhd->brjqhd', p[..., n_loc:], v_c))
    y_lat = o.reshape(bsz, seq, D_MODEL) @ w_out
    y_ctx = None
    if ctx_out:
        q_c = heads(h_ctx @ w_qkv[:, :D_MODEL])
        s_cc = jnp.einsum('bqhd,bkhd->bhqk', q_c, k_c).astype(jnp.float32) * scale
        p_cc = jax.nn.softmax(s_cc, axis=-1).astype(v_c.dtype)
        o_c = jnp.einsum('bhqk,bkhd->bqhd', p_cc, v_c)
        y_ctx = o_c.reshape(bsz, h_ctx.shape[1], D_MODEL) @ w_out
    return y_ctx, y_lat

def first_inputs(seed: int = 0) -> dict:
    key = jax.random.key(seed)
    keys = iter(jax.random.split(key, 32))
    f32 = jnp.float32

    def normal(shape, std):
        return jax.random.normal(next(keys), shape, f32) * std

    n_a, n_b, n_c, n_d = (_layers_of(m) for m in range(N_MIXERS))
    d = D_MODEL
    lam_shape = (n_c, 2, S5_GROUPS, S5_STATE)
    return {
        'x': normal((BATCH, SEQ, d), 1.0),
        'c': normal((BATCH, d), 1.0),
        'ctx': normal((BATCH, CTX_LEN, d), 1.0),
        'c_ctx': normal((d,), 1.0),
        'ada_w': normal((DEPTH, d, N_MOD * d), 0.5 * d ** -0.5),
        'ada_b': normal((DEPTH, N_MOD * d), 0.02),
        'norm_gains': 1.0 + normal((DEPTH, 4, d), 0.02),
        'mlp_w_in': normal((DEPTH, d, D_FF), d ** -0.5),
        'mlp_w_out': normal((DEPTH, D_FF, d), D_FF ** -0.5),
        'sc_w_in': normal((n_a, d, 3 * d), d ** -0.5),
        'sc_conv': normal((n_a, CONV_W, d), CONV_W ** -0.5),
        'sc_w_out': normal((n_a, d, d), d ** -0.5),
        'hg_w_in': normal((n_b, d, 5 * d), d ** -0.5),
        'hg_lower_bound': normal((DEPTH, d), 0.1),
        'hg_norm': 1.0 + normal((n_b, d), 0.02),
        'hg_w_out': normal((n_b, d, d), d ** -0.5),
        's5_lam_re': -0.5 + normal(lam_shape, 0.01),
        's5_lam_im': math.pi * jnp.arange(S5_STATE, dtype=f32) + normal(lam_shape, 0.01),
        's5_log_dt': jax.random.uniform(next(keys), (n_c, 2, S5_GROUPS), f32,
                                        math.log(S5_DT_MIN), math.log(S5_DT_MAX)),
        's5_b_re': normal((n_c, S5_GROUPS, S5_STATE, S5_GROUP), (2 * S5_GROUP) ** -0.5),
        's5_b_im': normal((n_c, S5_GROUPS, S5_STATE, S5_GROUP), (2 * S5_GROUP) ** -0.5),
        's5_c_re': normal((n_c, 2, S5_GROUPS, S5_GROUP, S5_STATE), (2 * S5_STATE) ** -0.5),
        's5_c_im': normal((n_c, 2, S5_GROUPS, S5_GROUP, S5_STATE), (2 * S5_STATE) ** -0.5),
        's5_d': normal((n_c, d), 1.0),
        's5_w_glu': normal((n_c, d, 2 * d), d ** -0.5),
        'na_w_qkv': normal((n_d, d, 3 * d), d ** -0.5),
        'na_rpb': normal((n_d, NA_HEADS, 2 * NA_ROWS - 1, 2 * NA_COLS - 1), 0.1),
        'na_w_out': normal((n_d, d, d), d ** -0.5),
    }

def first_block(x, c, ctx, c_ctx, ada_w, ada_b, norm_gains, mlp_w_in, mlp_w_out,
              sc_w_in, sc_conv, sc_w_out, hg_w_in, hg_lower_bound, hg_norm, hg_w_out,
              s5_lam_re, s5_lam_im, s5_log_dt, s5_b_re, s5_b_im, s5_c_re, s5_c_im, s5_d, s5_w_glu,
              na_w_qkv, na_rpb, na_w_out):
    lb_all = jnp.cumsum(jax.nn.softmax(hg_lower_bound.astype(jnp.float32), axis=0), axis=0)
    lb_all = lb_all - lb_all[0]
    h_lat, h_ctx = x, ctx
    for i in range(DEPTH):
        kind, j = i % N_MIXERS, i // N_MIXERS
        ctx_out = i < DEPTH - 1
        mod_lat = [m[:, None, :] for m in jnp.split(jax.nn.silu(c) @ ada_w[i] + ada_b[i], N_MOD, axis=-1)]
        mod_ctx = jnp.split(jax.nn.silu(c_ctx) @ ada_w[i] + ada_b[i], N_MOD, axis=-1)
        g_pre, g_post, g_pre_ff, g_post_ff = norm_gains[i]
        a_lat = modulate(rmsnorm(h_lat, g_pre), mod_lat[0], mod_lat[1])
        a_ctx = modulate(rmsnorm(h_ctx, g_pre), mod_ctx[0], mod_ctx[1]) if (ctx_out or kind != 0) else None
        if kind == 0:
            y_lat = short_gated_conv(a_lat, sc_w_in[j], sc_conv[j], sc_w_out[j])
            y_ctx = short_gated_conv(a_ctx, sc_w_in[j], sc_conv[j], sc_w_out[j]) if ctx_out else None
        elif kind == 1:
            y_ctx, y_lat = hgrn2_mixer(a_ctx, a_lat, hg_w_in[j], lb_all[i], hg_norm[j], hg_w_out[j], ctx_out)
        elif kind == 2:
            y_ctx, y_lat = s5_mixer(a_ctx, a_lat, s5_lam_re[j], s5_lam_im[j], s5_log_dt[j], s5_b_re[j],
                                    s5_b_im[j], s5_c_re[j], s5_c_im[j], s5_d[j], s5_w_glu[j], ctx_out)
        else:
            y_ctx, y_lat = neighbourhood_attention(a_ctx, a_lat, na_w_qkv[j], na_rpb[j], na_w_out[j], ctx_out)
        h_lat = h_lat + mod_lat[2] * rmsnorm(y_lat.astype(h_lat.dtype), g_post)
        if ctx_out:
            h_ctx = h_ctx + mod_ctx[2] * rmsnorm(y_ctx.astype(h_ctx.dtype), g_post)
        f_lat = squared_relu_mlp(modulate(rmsnorm(h_lat, g_pre_ff), mod_lat[3], mod_lat[4]), mlp_w_in[i], mlp_w_out[i])
        h_lat = h_lat + mod_lat[5] * rmsnorm(f_lat.astype(h_lat.dtype), g_post_ff)
        if ctx_out:
            f_ctx = squared_relu_mlp(modulate(rmsnorm(h_ctx, g_pre_ff), mod_ctx[3], mod_ctx[4]), mlp_w_in[i], mlp_w_out[i])
            h_ctx = h_ctx + mod_ctx[5] * rmsnorm(f_ctx.astype(h_ctx.dtype), g_post_ff)
    return h_lat


SG_WIDTH = 512
SG_GROUPS = 8
SG_GROUP_DIM = SG_WIDTH // SG_GROUPS
CHUNK = 128
CV_WIDTH = 512
CV_KERNEL = 31
SB_HEADS = 8
SB_HEAD_DIM = 64
SB_WIDTH = SB_HEADS * SB_HEAD_DIM
Q_BLOCK = 128
N_BRANCH = 3
D_FF_2 = 2816
FFN_KERNEL = 3

IN_COLS = 2 * SG_WIDTH + 2 * CV_WIDTH + 3 * SB_WIDTH + N_BRANCH * D_MODEL


def rms_norm(x, g):
    xf = x.astype(jnp.float32)
    y = xf * lax.rsqrt(jnp.mean(xf * xf, axis=-1, keepdims=True) + EPS)
    return (y * g.astype(jnp.float32)).astype(x.dtype)

def layer_norm(x, g, b):
    xf = x.astype(jnp.float32)
    mu = jnp.mean(xf, axis=-1, keepdims=True)
    xc = xf - mu
    y = xc * lax.rsqrt(jnp.mean(xc * xc, axis=-1, keepdims=True) + EPS)
    return (y * g.astype(jnp.float32) + b.astype(jnp.float32)).astype(x.dtype)

def causal_depthwise_conv(x, w, b):
    k_width, ch = w.shape
    y = lax.conv_general_dilated(
        x, w[:, None, :].astype(x.dtype), window_strides=(1,), padding=[(k_width - 1, 0)],
        dimension_numbers=("NWC", "WIO", "NWC"), feature_group_count=ch)
    return y + b.astype(x.dtype)

def chunked_spatial_gating(v, w_s, b_s):
    bsz, t, _ = v.shape
    vc = v.reshape(bsz, t // CHUNK, CHUNK, SG_GROUPS, SG_GROUP_DIM)
    tril = jnp.tril(jnp.ones((CHUNK, CHUNK), dtype=bool))
    w_m = jnp.where(tril[None], w_s, jnp.zeros_like(w_s)).astype(v.dtype)
    out = jnp.einsum("gts,bcsgd->bctgd", w_m, vc) + b_s.T.astype(v.dtype)[:, :, None]
    return out.reshape(bsz, t, SG_WIDTH)

def stick_breaking_attention(q, k, v):
    bsz, t, h, dh = q.shape
    q = q.transpose(0, 2, 1, 3)
    k = k.transpose(0, 2, 1, 3)
    v = v.transpose(0, 2, 1, 3)
    scale = 1.0 / math.sqrt(dh)
    outs = []
    for i in range(t // Q_BLOCK):
        ctx = (i + 1) * Q_BLOCK
        q_blk = q[:, :, i * Q_BLOCK:ctx]
        z = jnp.einsum("bhqd,bhkd->bhqk", q_blk, k[:, :, :ctx]).astype(jnp.float32) * scale
        q_pos = i * Q_BLOCK + jnp.arange(Q_BLOCK)
        k_pos = jnp.arange(ctx)
        mask = k_pos[None, :] < q_pos[:, None]
        log_1m_beta = jnp.where(mask, jax.nn.log_sigmoid(-z), 0.0)
        cs = lax.cumsum(log_1m_beta, axis=3)
        log_a = jax.nn.log_sigmoid(z) + (cs[..., -1:] - cs)
        a = jnp.where(mask, jnp.exp(log_a), 0.0)
        outs.append(jnp.einsum("bhqk,bhkd->bhqd", a.astype(v.dtype), v[:, :, :ctx]))
    o = jnp.concatenate(outs, axis=2)
    return o.transpose(0, 2, 1, 3).reshape(bsz, t, h * dh)

def second_inputs(seed: int = 0) -> dict:
    key = jax.random.key(seed)
    ks = jax.random.split(key, 24)
    f32 = jnp.float32
    L, D = DEPTH, D_MODEL

    def nrm(k, shape, scale):
        return jax.random.normal(k, shape, f32) * scale

    return {
        "x": jax.random.normal(ks[0], (BATCH, SEQ, D), f32),
        "ln1_g": 1.0 + nrm(ks[1], (L, D), 0.05),
        "w_in": nrm(ks[2], (L, D, IN_COLS), D ** -0.5),
        "b_gate": nrm(ks[3], (L, N_BRANCH, D), 0.1),
        "sg_ln_g": 1.0 + nrm(ks[4], (L, SG_WIDTH), 0.05),
        "sg_ln_b": nrm(ks[5], (L, SG_WIDTH), 0.05),
        "sg_w": nrm(ks[6], (L, SG_GROUPS, CHUNK, CHUNK), CHUNK ** -0.5),
        "sg_b": 1.0 + nrm(ks[7], (L, SG_GROUPS, CHUNK), 0.1),
        "w_a_out": nrm(ks[8], (L, SG_WIDTH, D), SG_WIDTH ** -0.5),
        "cv_w": nrm(ks[9], (L, CV_KERNEL, CV_WIDTH), CV_KERNEL ** -0.5),
        "cv_b": nrm(ks[10], (L, CV_WIDTH), 0.05),
        "cv_ln_g": 1.0 + nrm(ks[11], (L, CV_WIDTH), 0.05),
        "cv_ln_b": nrm(ks[12], (L, CV_WIDTH), 0.05),
        "w_b_out": nrm(ks[13], (L, CV_WIDTH, D), CV_WIDTH ** -0.5),
        "q_norm_g": 1.0 + nrm(ks[14], (L, SB_HEAD_DIM), 0.05),
        "k_norm_g": 1.0 + nrm(ks[15], (L, SB_HEAD_DIM), 0.05),
        "w_c_out": nrm(ks[16], (L, SB_WIDTH, D), SB_WIDTH ** -0.5),
        "w_out": nrm(ks[17], (L, D, D), D ** -0.5),
        "ln2_g": 1.0 + nrm(ks[18], (L, D), 0.05),
        "w_up": nrm(ks[19], (L, D, 2 * D_FF_2), D ** -0.5),
        "ffn_conv_w": nrm(ks[20], (L, FFN_KERNEL, 2 * D_FF_2), FFN_KERNEL ** -0.5),
        "ffn_conv_b": nrm(ks[21], (L, 2 * D_FF_2), 0.05),
        "w_down": nrm(ks[22], (L, D_FF_2, D), D_FF_2 ** -0.5),
    }

def second_block(x, ln1_g, w_in, b_gate, sg_ln_g, sg_ln_b, sg_w, sg_b, w_a_out,
              cv_w, cv_b, cv_ln_g, cv_ln_b, w_b_out, q_norm_g, k_norm_g, w_c_out,
              w_out, ln2_g, w_up, ffn_conv_w, ffn_conv_b, w_down):
    bsz, t, d = x.shape
    split_at = np.cumsum([2 * SG_WIDTH, 2 * CV_WIDTH, 3 * SB_WIDTH]).tolist()
    for l in range(DEPTH):
        h = rms_norm(x, ln1_g[l])
        z = h @ w_in[l]
        z_a, z_b, z_c, z_g = jnp.split(z, split_at, axis=-1)

        a = jax.nn.gelu(z_a)
        u, v = jnp.split(a, 2, axis=-1)
        v = layer_norm(v, sg_ln_g[l], sg_ln_b[l])
        y_a = (u * chunked_spatial_gating(v, sg_w[l], sg_b[l])) @ w_a_out[l]

        p, g_lin = jnp.split(z_b, 2, axis=-1)
        c = p * jax.nn.sigmoid(g_lin)
        c = causal_depthwise_conv(c, cv_w[l], cv_b[l])
        c = jax.nn.silu(layer_norm(c, cv_ln_g[l], cv_ln_b[l]))
        y_b = c @ w_b_out[l]

        q, k, vv = jnp.split(z_c, 3, axis=-1)
        q = rms_norm(q.reshape(bsz, t, SB_HEADS, SB_HEAD_DIM), q_norm_g[l])
        k = rms_norm(k.reshape(bsz, t, SB_HEADS, SB_HEAD_DIM), k_norm_g[l])
        vv = vv.reshape(bsz, t, SB_HEADS, SB_HEAD_DIM)
        y_c = stick_breaking_attention(q, k, vv) @ w_c_out[l]

        gates = jax.nn.sigmoid(z_g.reshape(bsz, t, N_BRANCH, d) + b_gate[l].astype(z_g.dtype))
        merged = gates[:, :, 0] * y_a + gates[:, :, 1] * y_b + gates[:, :, 2] * y_c
        x = x + merged @ w_out[l]

        h2 = rms_norm(x, ln2_g[l])
        up = causal_depthwise_conv(h2 @ w_up[l], ffn_conv_w[l], ffn_conv_b[l])
        gate, val = jnp.split(up, 2, axis=-1)
        x = x + (jax.nn.silu(gate) * val) @ w_down[l]
    return x


def setup_inputs(seed=0):
    out = dict(first_inputs(seed))
    for name, value in second_inputs(seed + 1).items():
        if name != "x":
            out[name + "_2"] = value
    return out


def reference(
    x, c, ctx, c_ctx, ada_w, ada_b, norm_gains, mlp_w_in, mlp_w_out, sc_w_in, sc_conv, sc_w_out,
    hg_w_in, hg_lower_bound, hg_norm, hg_w_out, s5_lam_re, s5_lam_im, s5_log_dt, s5_b_re,
    s5_b_im, s5_c_re, s5_c_im, s5_d, s5_w_glu, na_w_qkv, na_rpb, na_w_out, ln1_g_2, w_in_2,
    b_gate_2, sg_ln_g_2, sg_ln_b_2, sg_w_2, sg_b_2, w_a_out_2, cv_w_2, cv_b_2, cv_ln_g_2,
    cv_ln_b_2, w_b_out_2, q_norm_g_2, k_norm_g_2, w_c_out_2, w_out_2, ln2_g_2, w_up_2,
    ffn_conv_w_2, ffn_conv_b_2, w_down_2,
):
    x = first_block(
        x, c, ctx, c_ctx, ada_w, ada_b, norm_gains, mlp_w_in, mlp_w_out, sc_w_in, sc_conv,
        sc_w_out, hg_w_in, hg_lower_bound, hg_norm, hg_w_out, s5_lam_re, s5_lam_im, s5_log_dt,
        s5_b_re, s5_b_im, s5_c_re, s5_c_im, s5_d, s5_w_glu, na_w_qkv, na_rpb, na_w_out,
    )
    return second_block(
        x, ln1_g_2, w_in_2, b_gate_2, sg_ln_g_2, sg_ln_b_2, sg_w_2, sg_b_2, w_a_out_2, cv_w_2,
        cv_b_2, cv_ln_g_2, cv_ln_b_2, w_b_out_2, q_norm_g_2, k_norm_g_2, w_c_out_2, w_out_2,
        ln2_g_2, w_up_2, ffn_conv_w_2, ffn_conv_b_2, w_down_2,
    )


_drawn_inputs = setup_inputs


def setup_inputs(seed=0):
    import zlib

    import numpy as np

    out = dict(_drawn_inputs(seed))
    spreads = {}
    factors = {'norm_gains': 3.254,
     'sg_ln_g_2': 5.315,
     'sg_ln_b_2': 5.315,
     'cv_ln_g_2': 3.289,
     'cv_ln_b_2': 3.702,
     'q_norm_g_2': 8.0,
     'k_norm_g_2': 8.0,
     'sg_b_2': 4.047,
     'ln2_g_2': 3.416,
     'ffn_conv_b_2': 3.532}
    for name, (base, spread) in spreads.items():
        noise = np.random.default_rng([zlib.crc32(name.encode()), seed]).standard_normal(out[name].shape)
        drawn = base * np.exp(spread * noise) if base else spread * noise
        out[name] = jnp.asarray(drawn.astype(out[name].dtype))
    for name, factor in factors.items():
        out[name] = (out[name] * factor).astype(out[name].dtype)
    return out
```

```python
import concourse.bass as bass
from concourse import mybir
from contextlib import ExitStack, contextmanager

P = 128
T = 256
D = 1024
DT = D // P
RAW_SLOTS = 4
SPLIT_SLOTS = 4
AHEAD = SPLIT_SLOTS - 1
UNIT = 2048
EPS = 1e-6
SG = 512
CV_TAPS = 31
HEADS = 8

STAGES = [("sc_in", 16, 12), ("sc_out", 4, 16), ("mlp_in", 16, 16), ("mlp_out", 16, 16),
          ("z_in", 26, 16), ("branch", 8, 12), ("mix_out", 4, 16), ("up", 22, 16), ("down", 16, 11)]
N_BLOCKS = {name: n for name, n, _ in STAGES}
WORDS = {name: t * P for name, _, t in STAGES}
FIRST = {}
STAGE_OF = []
for _name, _n, _ in STAGES:
    FIRST[_name] = len(STAGE_OF)
    STAGE_OF += [_name] * _n
ADA_FIRST = 8
ADA_AFTER = {"sc_in": range(0, 16), "sc_out": range(16, 20), "mlp_out": range(40, 44)}
CREDIT = {"sc_in": 2, "mlp_in": 4, "mlp_out": 2, "branch": 2, "up": 4}
Z_ORDER = ["q", "q", "k", "k", "vv", "vv"] + ["pg"] * 4 + ["v", "v", "u", "u"] + ["gate"] * 12
PARAMS = [("c", 8), ("ada_b", 48), ("gains", 32), ("sc_conv", 24), ("ln1", 8), ("b_gate", 24),
          ("cv_w", 4 * CV_TAPS), ("cv_b", 4), ("cv_g", 4), ("cv_lb", 4), ("qk_g", 2), ("ln2", 8),
          ("up_w", 132), ("up_b", 44)]
PCOL = {}
_at = 0
for _name, _n in PARAMS:
    PCOL[_name] = _at
    _at += _n
N_PARAMS = _at
N_CONST = 10
Z_FILL = {s: n for n, s in enumerate(s for s, kind in enumerate(Z_ORDER) if kind not in ("v", "vv"))}
VLN_STEP, SG_STEP = 13, 14
QK_STEP = lambda p: 13 + 2 * p
U_STEP = lambda p: 15 + 2 * p
AV_STEP = lambda p: 16 + 2 * p
CONV_STEPS, CONV_PER_STEP = range(8, 22), 9
CV_MEAN_STEP, CV_VAR_STEP = 22, 23


def raw_unit(block):
    return ADA_FIRST + block + sum(min(max(block - r.start, 0), len(r)) for r in ADA_AFTER.values())


def has_ada(block):
    return any(block in r for r in ADA_AFTER.values())


class Chain:

    def __init__(self, eng, sem):
        self.eng, self.sem, self.n, self.base = eng, sem, 0, 0

    def mark(self, ins):
        ins.then_inc(self.sem, 1)
        self.n += 1
        return self.n

    def wait(self, n=None):
        self.eng.wait_ge(self.sem, self.base + (self.n if n is None else n))

    def link(self, ins):
        self.mark(ins)
        self.wait()

    @contextmanager
    def loop(self, first, end, per):
        start = self.n
        with self.eng.Fori(first, end) as it:
            self.base = it * per - first * per
            yield it
        assert self.n == start + per, self.n - start
        self.n, self.base = start + (end - first) * per, 0


def build_program(nc, x_in, params, ada, ada_half, w, wm_t, sg_bias, sg_ln, out):
    f32, f32r = mybir.dt.float32, mybir.dt.float32r
    ALU, ACT = mybir.AluOpType, mybir.ActivationFunctionType
    ADD, SUB, MUL, MAX = ALU.add, ALU.subtract, ALU.mult, ALU.max
    ctx = ExitStack()
    with ctx:
        def sb(name, shape, dt=f32, c=ctx):
            return c.enter_context(nc.sbuf_tensor(name, shape, dt))

        def sem(name):
            return ctx.enter_context(nc.semaphore(name))

        raw = sb("raw", [P, RAW_SLOTS, UNIT])
        w_hi = sb("w_hi", [P, SPLIT_SLOTS, UNIT], f32r)
        w_lo = sb("w_lo", [P, SPLIT_SLOTS, UNIT], f32r)
        par = sb("par", [P, N_PARAMS])
        x = sb("x", [P, DT, T])
        a_hi = sb("a_hi", [P, DT, T], f32r)
        a_lo = sb("a_lo", [P, DT, T], f32r)
        y = sb("y", [P, DT, T])
        sq = sb("sq", [P, 2, 2 * T])
        std = sb("std", [P, 2 * T])
        rstd = sb("rstd", [P, 2 * T])
        mod = sb("mod", [P, 48])
        silu_c = sb("silu_c", [P, DT])
        gain_pre = sb("gain_pre", [P, DT])
        gain_post = sb("gain_post", [P, DT])
        gain_pre_ff = sb("gain_pre_ff", [P, DT])
        gain_post_ff = sb("gain_post_ff", [P, DT])
        qk_gain = sb("qk_gain", [P, 2])
        eps = sb("eps", [P, 1])
        ones = sb("ones", [P, P])

        with ExitStack() as c:
            ada_acc = sb("ada_acc", [P, 5, D], c=c)
            sc_hi = sb("sc_hi", [P, DT, T], f32r, c=c)
            sc_lo = sb("sc_lo", [P, DT, T], f32r, c=c)
            sc_c = sb("sc_c", [P, 2, T], c=c)
            sc_cv = sb("sc_cv", [P, 2, T + 2], c=c)
            sc_u = sb("sc_u", [P, 2, T], c=c)
            sc_y = sb("sc_y", [P, 2, T], c=c)
        with ExitStack() as c:
            hid_hi = sb("hid_hi", [P, 32, T], f32r, c=c)
            hid_lo = sb("hid_lo", [P, 32, T], f32r, c=c)
            hid = sb("hid", [P, 2, 2 * T], c=c)
        with ExitStack() as c:
            br = {}
            for name in ("a", "c"):
                br[name] = [sb(f"br_{name}_{part}", [P, 4, T], f32r, c=c) for part in ("hi", "lo")]
            cacc = sb("cacc", [P, 4, T], c=c)
            vv = sb("vv", [P, 2, SG], c=c)
            head_ones = sb("head_ones", [P, P], c=c)
            neg_upper = sb("neg_upper", [P, P], c=c)
            neg_ones = sb("neg_ones", [P, P], c=c)
            bn = sb("bn", [P, 2, 8], c=c)
            vstd = sb("vstd", [P, 4], c=c)
            with ExitStack() as early:
                sig = sb("sig", [P, 2, T], c=early)
                sb("unused_gates_head", [P, 4, T], c=early)
                sgo = sb("sgo", [P, 4, T], c=early)
                vg = sb("vg", [P, 2, SG], c=early)
                wm = sb("wm", [P, HEADS, P], c=early)
                sgb = sb("sgb", [P, 4, P], c=early)
                sgln = sb("sgln", [P, 2, SG], c=early)
            gates = sb("gates", [P, 24, T], c=c)
            with ExitStack() as early:
                cpad = sb("cpad", [P, 4, T + CV_TAPS - 1], c=early)
                sp_t = sb("sp_t", [P, 2, 384], c=early)
            br["b"] = [sb(f"br_b_{part}", [P, 4, T], f32r, c=c) for part in ("hi", "lo")]
            with ExitStack() as late:
                mg_t = sb("mg_t", [P, 3, T], c=late)
            sp = sb("sp", [P, 2, 512], c=c)
            with ExitStack() as early:
                u_sb = sb("u_sb", [P, 4, T], c=early)
            att = sb("att", [P, 2, 512], c=c)
        with ExitStack() as c:
            up_hi = sb("up_hi", [P, 22, T], f32r, c=c)
            up_lo = sb("up_lo", [P, 22, T], f32r, c=c)
            up_u = sb("up_u", [P, 2, 2 * T], c=c)
            up_g = sb("up_g", [P, 2, T], c=c)
            up_p = sb("up_p", [P, 2, T], c=c)

        ps = ctx.enter_context(nc.psum_tensor("ps", [P, 8, 2 * T], f32))
        STAT, MISC = 4, 5
        TOKEN_BANK = 2
        SG_BANK = 6
        Z_BANKS = [2, 6]

        raw_in = [sem(f"raw_in{i}") for i in range(RAW_SLOTS)]
        raw_used = sem("raw_used")
        w_high = sem("w_high")
        w_used = sem("w_used")
        free = {s: sem(f"free_{s}") for s in CREDIT}
        par_in = sem("par_in")
        x_landed = sem("x_landed")
        z_const_in = sem("z_const_in")
        const_set = sem("const_set")
        c_ready = sem("c_ready")
        mod_ps = sem("mod_ps")
        mod_read = sem("mod_read")
        sq_ready = sem("sq_ready")
        sq_used = sem("sq_used")
        std_ready = sem("std_ready")
        std_used = sem("std_used")
        norm_t = sem("norm_t")
        act_hi = sem("act_hi")
        act_lo = sem("act_lo")
        x_new = sem("x_new")
        sc_c_ready = sem("sc_c_ready")
        sc_ready = sem("sc_ready")
        hid_ready = sem("hid_ready")
        hid_split = sem("hid_split")
        z_free_dve = sem("z_free_dve")
        z_free_act = sem("z_free_act")
        qk_ready = sem("qk_ready")
        vv_ready = sem("vv_ready")
        sig_ready = sem("sig_ready")
        c_in = sem("c_in")
        conv_step = sem("conv_step")
        vg_ready = sem("vg_ready")
        vg_var = sem("vg_var")
        vg_std = sem("vg_std")
        vln_ready = sem("vln_ready")
        wm_ready = sem("wm_ready")
        sg_done = sem("sg_done")
        br_a = sem("br_a")
        br_b = sem("br_b")
        br_c = sem("br_c")
        z_done = sem("z_done")
        sp_log = sem("sp_log")
        sp_ready = sem("sp_ready")
        sp_masked = sem("sp_masked")
        loga_done = sem("loga_done")
        loga_low = sem("loga_low")
        att_exp = sem("att_exp")
        att_ready = sem("att_ready")
        att_done = sem("att_done")
        cv_mean = sem("cv_mean")
        cv_cent = sem("cv_cent")
        cv_norm = sem("cv_norm")
        cv_silu = sem("cv_silu")
        gates_ready = sem("gates_ready")
        mix_ready = sem("mix_ready")
        up_u_ready = sem("up_u_ready")
        up_g_ready = sem("up_g_ready")
        up_ready = sem("up_ready")
        act_self = sem("act_self")
        dve_self = sem("dve_self")
        out_ready = sem("out_ready")
        out_sem = sem("out_sem")

        def pcol(name, i=0, n=1):
            return par[:, PCOL[name] + i:PCOL[name] + i + n]

        def pdyn(name, i):
            return pcol(name, i) if isinstance(i, int) else par[:, bass.ds(i + PCOL[name], 1)]

        def row(t, i):
            return t[:, i, :]

        def landed_at(unit):
            return 16 * (unit // RAW_SLOTS + 1)

        def flat(t):
            return t.rearrange("p a b -> p (a b)")

        SQ = {"x": 0, "post": 4, "pre_ff": 8, "post_ff": 12, "ln1": 16, "qk": 20, "cv": 24, "ln2": 26}
        STATN = {"x": 0, "post": 1, "pre_ff": 2, "post_ff": 3, "ln1": 4, "qk": 5, "cv": 9, "ln2": 10}
        ACT_TILE = {"x": 0, "pre_ff": 8, "ln1": 16, "ln2": 24}
        X_NEW = {"pre_ff": 0, "ln1": 8, "ln2": 16}
        USED = SPLIT_SLOTS

        block = ctx.enter_context(nc.Block())

        @block.sync
        def _(sp_eng):
            e = sp_eng
            e.dma_start(par[:, :], params[:, :]).then_inc(par_in, 16)

            def load(unit_wait, slot, words, src):
                if unit_wait is not None:
                    e.wait_ge(raw_used, unit_wait)
                e.dma_start(raw[:, slot, 0:words], src).then_inc(raw_in[slot], 16)

            for i in range(ADA_FIRST):
                load(i - RAW_SLOTS + 1 if i >= RAW_SLOTS else None, i % RAW_SLOTS, UNIT, ada[i])
                if i == 0:
                    e.dma_start(x[:, :, :], x_in).then_inc(x_landed, 16)
            ada_next = ADA_FIRST
            for s, n, _ in STAGES:
                u0 = raw_unit(FIRST[s])
                if s == "sc_in":
                    with e.Fori(0, n // 4) as it:
                        for b in range(4):
                            u = u0 + 2 * b
                            load(it * 8 + (u - RAW_SLOTS + 1), u % RAW_SLOTS, WORDS[s], w[s][it * 4 + b])
                            load(it * 8 + (u - RAW_SLOTS + 2), (u + 1) % RAW_SLOTS, D, ada_half[it * 4 + b])
                    continue
                m = n // 4 if s not in ADA_AFTER else 0
                if m:
                    with e.Fori(0, m) as it:
                        for b in range(4):
                            load(it * 4 + (u0 + b - RAW_SLOTS + 1), (u0 + b) % RAW_SLOTS, WORDS[s], w[s][it * 4 + b])
                for j in range(4 * m, n):
                    u = raw_unit(FIRST[s] + j)
                    load(u - RAW_SLOTS + 1, u % RAW_SLOTS, WORDS[s], w[s][j])
                    if has_ada(FIRST[s] + j):
                        load(u - RAW_SLOTS + 2, (u + 1) % RAW_SLOTS, UNIT, ada[ada_next])
                        ada_next += 1
            for t in range(4):
                e.wait_ge(out_ready, t + 1)
                e.dma_start(out[:, 2 * t:2 * t + 2, :], x[:, 2 * t:2 * t + 2, :]).then_inc(out_sem, 16)
            e.wait_ge(out_sem, 64)

        @block.gpsimd
        def _(pool):
            e = pool
            e.sem_inc(w_used, USED)
            for s, n in CREDIT.items():
                e.sem_inc(free[s], n)
            def constant(ins, n):
                ins.then_inc(const_set, 1)
                e.wait_ge(const_set, n)

            constant(e.memset(eps[:, :], EPS), 1)
            constant(e.memset(ones[:, :], 1.0), 2)
            constant(e.memset(flat(ada_acc[:, 2:4, :]), 0.0), 3)
            constant(e.memset(sc_cv[:, :, :], 0.0), 4)
            e.wait_ge(w_used, USED + FIRST["z_in"])
            e.dma_start(wm[:, :, :], wm_t).then_inc(z_const_in, 16)
            e.dma_start(sgb[:, :, :], sg_bias).then_inc(z_const_in, 16)
            e.dma_start(sgln[:, :, :], sg_ln).then_inc(z_const_in, 16)
            constant(e.memset(head_ones[:, :], 0.0), 5)
            constant(e.memset(head_ones[0:64, 0:64], 1.0), 6)
            constant(e.memset(head_ones[64:128, 64:128], 1.0), 7)
            constant(e.memset(neg_ones[:, :], -1.0), 8)
            constant(e.memset(neg_upper[:, :], -1.0), 9)
            constant(e.affine_select(out=neg_upper[:, :], in_=neg_upper[:, :], pattern=[[-1, P]],
                                     compare_op=ALU.is_ge, fill=0.0, base=0, channel_multiplier=1), 10)
            e.wait_ge(z_const_in, 48)
            e.memset(cpad[:, :, 0:CV_TAPS - 1], 0.0).then_inc(wm_ready, 1)
            e.wait_ge(wm_ready, 1)
            e.affine_select(out=wm[:, :, :], in_=wm[:, :, :], pattern=[[0, HEADS], [1, P]], compare_op=ALU.is_ge,
                            fill=0.0, base=0, channel_multiplier=-1).then_inc(wm_ready, 1)

            e.wait_ge(wm_ready, 2)

            def mask(t, ready, n):
                v = t[:, :, :].rearrange("p h (a b) -> p h a b", a=2)[:, :, :, 0:P]
                e.affine_select(out=v, in_=v, pattern=[[0, 2], [0, 2], [1, P]], compare_op=ALU.is_gt,
                                fill=0.0, base=0, channel_multiplier=-1).then_inc(ready, 1)
                e.wait_ge(ready, n)

            for p in range(4):
                e.wait_ge(sp_ready, p + 1)
                mask(sp, sp_masked, p + 1)
                e.wait_ge(att_exp, p + 1)
                mask(att, att_ready, p + 1)

        @block.scalar
        def _(act):
            e = act
            ch = Chain(e, act_self)

            def high(g, static_g, words, landed):
                slot, unit_slot = static_g % SPLIT_SLOTS, raw_unit(static_g) % RAW_SLOTS
                e.wait_ge(raw_in[unit_slot], landed)
                e.wait_ge(w_used, g + 1)
                e.activation(w_hi[:, slot, 0:words], raw[:, unit_slot, 0:words], ACT.Copy).then_inc(w_high, 1)

            def high_at(g):
                if g < len(STAGE_OF):
                    high(g, g, WORDS[STAGE_OF[g]], landed_at(raw_unit(g)))

            def run(stage, step, per=0):
                n, g0 = N_BLOCKS[stage], FIRST[stage]
                last = max((n - 4) // 4, 1)
                k = 2 if stage == "sc_in" else 1
                for b in range(4):
                    high_at(g0 + b + AHEAD)
                    step(0, b)
                if last > 1:
                    with ch.loop(1, last, per) as it:
                        for b in range(4):
                            g = g0 + b + AHEAD
                            high(it * 4 + g, g, WORDS[stage], it * (16 * k) + landed_at(raw_unit(g)))
                            step(it, b)
                for j in range(4 * last, n):
                    high_at(g0 + j + AHEAD)
                    step(j // 4, j % 4)

            def square(number, src):
                if number >= 2:
                    e.wait_ge(sq_used, number - 1)
                e.activation(sq[:, number % 2, :], src, ACT.Square).then_inc(sq_ready, 1)

            def deviation(number, pairs_summed, width, count):
                e.wait_ge(sq_used, pairs_summed)
                if number >= 1:
                    e.wait_ge(std_used, number)
                e.activation(std[:, 0:width], ps[:, STAT, 0:width], ACT.Sqrt, bias=eps[:, :],
                             scale=1.0 / count).then_inc(std_ready, 1)

            def act_high(norm, shift):
                for i in range(DT):
                    e.wait_ge(norm_t, ACT_TILE[norm] + i + 1)
                    if shift is None:
                        ins = e.activation(a_hi[:, i, :], y[:, i, :], ACT.Copy)
                    else:
                        ins = e.activation(a_hi[:, i, :], y[:, i, :], ACT.Identity,
                                           bias=mod[:, shift * DT + i:shift * DT + i + 1])
                    ins.then_inc(act_hi, 1)

            def x_norm(norm, shift):
                for t in range(4):
                    e.wait_ge(x_new, X_NEW[norm] + 2 * t + 2)
                    square(SQ[norm] + t, flat(x[:, 2 * t:2 * t + 2, :]))
                deviation(STATN[norm], SQ[norm] + 4, T, D)
                act_high(norm, shift)

            e.wait_ge(par_in, 16)
            e.wait_ge(const_set, 1)
            e.activation(silu_c[:, :], pcol("c", 0, 8), ACT.Silu).then_inc(c_ready, 1)
            e.wait_ge(x_landed, 16)
            for t in range(4):
                square(SQ["x"] + t, flat(x[:, 2 * t:2 * t + 2, :]))
            deviation(STATN["x"], SQ["x"] + 4, T, D)
            high_at(0)
            e.wait_ge(mod_read, 2)
            act_high("x", 0)
            for g in range(1, AHEAD):
                high_at(g)

            def sc_in_step(it, b):
                if b % 2 == 0:
                    return
                grp = it * 2 + b // 2
                e.wait_ge(w_used, it * 4 + b + 1 + FIRST["sc_in"] + USED)
                e.activation(sc_c[:, b // 2, :], ps[:, 2 * (b // 2), 0:T], ACT.Copy).then_inc(sc_c_ready, 1)

            run("sc_in", sc_in_step)

            def sc_out_step(it, b):
                j = 4 * it + b
                e.wait_ge(w_used, FIRST["sc_out"] + j + 1 + USED)
                square(SQ["post"] + j, ps[:, b, :])

            run("sc_out", sc_out_step)
            deviation(STATN["post"], SQ["post"] + 4, T, D)
            x_norm("pre_ff", 3)

            def mlp_in_step(it, b):
                e.wait_ge(w_used, it * 4 + (FIRST["mlp_in"] + b + 1 + USED))
                if not (isinstance(it, int) and 4 * it + b < 2):
                    e.wait_ge(hid_split, it * 4 + (b - 1))
                e.activation(hid[:, b % 2, :], ps[:, b, :], ACT.Relu).then_inc(free["mlp_in"], 1)
                e.wait_ge(free["mlp_in"], it * 4 + (b + 1 + CREDIT["mlp_in"]))
                e.activation(hid[:, b % 2, :], hid[:, b % 2, :], ACT.Square).then_inc(hid_ready, 1)

            run("mlp_in", mlp_in_step)

            def mlp_out_step(it, b):
                if b == 3:
                    e.wait_ge(w_used, it * 4 + (FIRST["mlp_out"] + b + 1 + USED))
                    square(SQ["post_ff"] + it, ps[:, it % 2, :])

            for j in range(N_BLOCKS["mlp_out"]):
                high_at(FIRST["mlp_out"] + j + AHEAD)
                mlp_out_step(j // 4, j % 4)
            deviation(STATN["post_ff"], SQ["post_ff"] + 4, T, D)
            x_norm("ln1", None)

            def softplus_log(p):
                zb = Z_BANKS[p % 2]
                e.wait_ge(z_done, p + 1)
                if p:
                    e.wait_ge(sp_ready, p)
                ch.link(e.activation(sp_t[:, :, :], ps[:, zb:zb + 2, 0:384], ACT.Abs))
                ch.link(e.activation(sp_t[:, :, :], sp_t[:, :, :], ACT.Exp, scale=-1.0))
                e.activation(sp_t[:, :, :], sp_t[:, :, :], ACT.Ln, bias=1.0).then_inc(sp_log, 1)

            def weights(p):
                e.wait_ge(loga_low, p + 1)
                e.activation(att[:, :, 0:384], att[:, :, 0:384], ACT.Exp).then_inc(att_exp, 1)

            for s, kind in enumerate(Z_ORDER):
                g = FIRST["z_in"] + s
                high_at(g + AHEAD)
                bank = Z_FILL[s] % 2 if s in Z_FILL else None
                if kind in ("q", "k", "pg", "u", "gate"):
                    e.wait_ge(w_used, g + 1 + USED)
                if kind in ("q", "k"):
                    square(SQ["qk"] + s, ps[:, bank, :])
                if 1 <= s <= 4:
                    deviation(STATN["qk"] + s - 1, SQ["qk"] + s, 2 * T, 64)
                if kind == "pg":
                    i = s - Z_ORDER.index("pg")
                    if i >= 2:
                        e.wait_ge(c_in, i - 1)
                    e.activation(sig[:, i % 2, :], ps[:, bank, T:2 * T], ACT.Sigmoid).then_inc(sig_ready, 1)
                if kind == "v" and Z_ORDER[s + 1] != "v":
                    e.wait_ge(w_used, g + 1 + USED)
                    for c in range(2):
                        e.activation(vg[:, c, :], ps[:, TOKEN_BANK + c, :], ACT.Gelu_apprx_tanh).then_inc(vg_ready, 1)
                if kind == "u":
                    i = s - Z_ORDER.index("u")
                    e.activation(flat(u_sb[:, 2 * i:2 * i + 2, :]), ps[:, bank, :],
                                 ACT.Gelu_apprx_tanh).then_inc(z_free_act, 1)
                if s == VLN_STEP:
                    e.wait_ge(vg_var, 2)
                    for c in range(2):
                        e.activation(vstd[:, c:c + 1], bn[:, c, 7:8], ACT.Sqrt, bias=eps[:, :]).then_inc(vg_std, 1)
                if kind == "gate":
                    for h in range(2):
                        n = 2 * (s - Z_ORDER.index("gate")) + h
                        ins = e.activation(gates[:, n, :], ps[:, bank, h * T:(h + 1) * T], ACT.Identity,
                                           bias=pcol("b_gate", n))
                        ch.mark(ins) if h == 0 else ins.then_inc(z_free_act, 1)
                for p in range(4):
                    if s == U_STEP(p):
                        weights(p)
                for p in range(4):
                    if s == QK_STEP(p):
                        softplus_log(p)
                if s == CV_VAR_STEP:
                    for t in range(2):
                        e.wait_ge(cv_cent, 2 * t + 2)
                        square(SQ["cv"] + t, flat(cacc[:, 2 * t:2 * t + 2, :]))
                    deviation(STATN["cv"], SQ["cv"] + 2, T, SG)
                    for i in range(4):
                        e.wait_ge(cv_norm, i + 1)
                        e.activation(cacc[:, i, :], cacc[:, i, :], ACT.Silu, bias=pcol("cv_lb", i)).then_inc(cv_silu, 1)
            e.wait_ge(z_free_act, 14)
            ch.wait()
            e.activation(flat(gates[:, 0:6, :]), flat(gates[:, 0:6, :]), ACT.Sigmoid).then_inc(gates_ready, 1)
            e.activation(flat(gates[:, 6:24, :]), flat(gates[:, 6:24, :]), ACT.Sigmoid).then_inc(gates_ready, 1)

            for s in ("branch", "mix_out"):
                for j in range(N_BLOCKS[s]):
                    high_at(FIRST[s] + j + AHEAD)
            x_norm("ln2", None)

            def silu_gate(it, b):
                e.wait_ge(free["up"], it * 4 + (b + 1 + CREDIT["up"]))
                if not (isinstance(it, int) and 4 * it + b < 2):
                    e.wait_ge(up_ready, it * 4 + (b - 1))
                e.activation(up_g[:, b % 2, :], up_u[:, b % 2, 0:T], ACT.Silu).then_inc(up_g_ready, 1)

            def up_step(it, b):
                e.wait_ge(w_used, it * 4 + (FIRST["up"] + b + 1 + USED))
                if not (isinstance(it, int) and 4 * it + b < 2):
                    e.wait_ge(up_ready, it * 4 + (b - 1))
                for h in range(2):
                    e.activation(up_u[:, b % 2, h * T:(h + 1) * T], ps[:, b, h * T:(h + 1) * T], ACT.Identity,
                                 bias=pdyn("up_b", it * 8 + (2 * b + h)),
                                 scale=pdyn("up_w", it * 24 + (3 * (2 * b + h) + 2))).then_inc(up_u_ready, 1)
                if isinstance(it, int):
                    if 4 * it + b >= 1:
                        silu_gate((4 * it + b - 1) // 4, (b - 1) % 4)
                else:
                    silu_gate(it - 1, 3) if b == 0 else silu_gate(it, b - 1)

            run("up", up_step)
            silu_gate(5, 1)
            for j in range(N_BLOCKS["down"]):
                high_at(FIRST["down"] + j + AHEAD)

        @block.vector
        def _(dve):
            e = dve
            ch = Chain(e, dve_self)

            def low(g, static_g, words):
                slot, unit_slot = static_g % SPLIT_SLOTS, raw_unit(static_g) % RAW_SLOTS
                e.wait_ge(w_high, g + 1)
                e.tensor_tensor(w_lo[:, slot, 0:words], raw[:, unit_slot, 0:words],
                                w_hi[:, slot, 0:words].bitcast(f32), SUB).then_inc(raw_used, 1)

            def ada_part(src, col, acc):
                return e.scalar_tensor_tensor(acc, src, col, acc, MUL, ADD)

            def ada_unit(u, k, acc):
                e.wait_ge(raw_in[u % RAW_SLOTS], landed_at(u))
                if u:
                    e.wait_ge(raw_used, u)
                src = raw[:, u % RAW_SLOTS, :]
                if k == 0:
                    ch.link(e.tensor_scalar(acc, src[:, 0:D], silu_c[:, 0:1], None, MUL))
                else:
                    ch.link(ada_part(src[:, 0:D], silu_c[:, k:k + 1], acc))
                ada_part(src[:, D:2 * D], silu_c[:, k + 1:k + 2], acc).then_inc(raw_used, 1)

            def ada_half_unit(unit, static_unit, landed, acc, col):
                e.wait_ge(raw_in[static_unit % RAW_SLOTS], landed)
                e.wait_ge(raw_used, unit)
                ada_part(raw[:, static_unit % RAW_SLOTS, 0:D], col, acc).then_inc(raw_used, 1)

            def ahead_at(g):
                if g < len(STAGE_OF):
                    low(g, g, WORDS[STAGE_OF[g]])
                u = raw_unit(g) + 1
                if g in ADA_AFTER["sc_in"]:
                    ada_half_unit(u, u, landed_at(u), ada_acc[:, 2 + g % 2, :], silu_c[:, g // 2:g // 2 + 1])
                if g in ADA_AFTER["sc_out"]:
                    ada_unit(u, 2 * (g - 16), ada_acc[:, 4, :])
                if g in ADA_AFTER["mlp_out"]:
                    ada_unit(u, 2 * (g - 40), hid[:, :, :].rearrange("p a b -> p (a b)"))

            def run(stage, step, per=0):
                n, g0 = N_BLOCKS[stage], FIRST[stage]
                last = max((n - 4) // 4, 1)
                for b in range(4):
                    ahead_at(g0 + b + AHEAD)
                    step(0, b)
                if last > 1:
                    with ch.loop(1, last, per) as it:
                        for b in range(4):
                            g = g0 + b + AHEAD
                            low(it * 4 + g, g, WORDS[stage])
                            if stage == "sc_in":
                                u = raw_unit(g) + 1
                                ada_half_unit(it * 8 + u, u, it * 32 + landed_at(u), ada_acc[:, 2 + g % 2, :],
                                              silu_c[:, bass.ds(it * 2 + g // 2, 1)])
                            step(it, b)
                for j in range(4 * last, n):
                    ahead_at(g0 + j + AHEAD)
                    step(j // 4, j % 4)

            def invert(number, width):
                e.wait_ge(std_ready, number + 1)
                e.reciprocal(rstd[:, 0:width], std[:, 0:width]).then_inc(std_used, 1)
                e.wait_ge(std_used, number + 1)

            def split(hi, lo, src, ready):
                ch.link(e.tensor_copy(hi, src))
                e.tensor_tensor(lo, src, hi.bitcast(f32), SUB).then_inc(ready, 1)

            def low_part(norm, i, shift):
                e.wait_ge(act_hi, ACT_TILE[norm] + i + 1)
                e.scalar_tensor_tensor(a_lo[:, i, :], y[:, i, :],
                                       0.0 if shift is None else mod[:, shift * DT + i:shift * DT + i + 1],
                                       a_hi[:, i, :].bitcast(f32), ADD, SUB).then_inc(act_lo, 1)

            def normalise(norm, gain, shift):
                for i in range(DT):
                    e.scalar_tensor_tensor(y[:, i, :], x[:, i, :], gain(i), rstd[:, 0:T], MUL, MUL).then_inc(norm_t, 1)
                    if i >= 2:
                        low_part(norm, i - 2, shift)
                low_part(norm, DT - 2, shift)
                low_part(norm, DT - 1, shift)

            def post_norm(gain):
                start = ch.n
                for i in range(DT + 1):
                    if i < DT:
                        ch.mark(e.scalar_tensor_tensor(y[:, i, :], y[:, i, :], gain[:, i:i + 1], rstd[:, 0:T], MUL, MUL))
                    if i >= 1:
                        ch.wait(start + i)
                        ins = e.tensor_tensor(x[:, i - 1, :], x[:, i - 1, :], y[:, i - 1, :], ADD)
                        ins.then_inc(x_new, 1)

            MOD_SUMMED = (1, 2, 5, 5, 5, 6)

            def mods(number, vector):
                e.wait_ge(mod_ps, MOD_SUMMED[number])
                cols = slice(8 * vector, 8 * vector + 8)
                e.tensor_tensor(mod[:, cols], ps[:, MISC, cols], pcol("ada_b", 8 * vector, 8), ADD).then_inc(mod_read, 1)
                e.wait_ge(mod_read, number + 1)

            e.wait_ge(c_ready, 1)
            for i in range(4):
                ada_unit(i, 2 * i, ada_acc[:, 1, :])
            invert(STATN["x"], T)
            for i in range(2):
                ada_unit(4 + i, 2 * i, ada_acc[:, 0, :])
            mods(0, 1)
            ch.link(e.scalar_tensor_tensor(gain_pre[:, :], mod[:, 8:16], 1.0, pcol("gains", 0, 8), ADD, MUL))
            for i in range(DT):
                e.scalar_tensor_tensor(y[:, i, :], x[:, i, :], gain_pre[:, i:i + 1], rstd[:, 0:T], MUL, MUL)\
                 .then_inc(norm_t, 1)
            for i in range(2, 4):
                ada_unit(4 + i, 2 * i, ada_acc[:, 0, :])
            e.wait_ge(const_set, 4)
            ahead_at(0)
            mods(1, 0)
            for i in range(DT):
                low_part("x", i, 0)
            for g in range(1, AHEAD):
                ahead_at(g)

            def sc_in_step(it, b):
                if b % 2 == 0:
                    return
                grp, pb = it * 2 + b // 2, b // 2
                tap = lambda t: pdyn("sc_conv", it * 6 + (3 * pb + t))
                u, cv = sc_u[:, pb, :], sc_cv[:, pb, :]
                e.wait_ge(sc_c_ready, grp + 1)
                ch.link(e.tensor_tensor(cv[:, 1:T + 1], ps[:, 2 * pb, T:2 * T], sc_c[:, pb, :], MUL))
                ch.link(e.tensor_scalar(u, cv[:, 1:T + 1], tap(1), None, MUL))
                ch.link(e.scalar_tensor_tensor(u, cv[:, 0:T], tap(0), u, MUL, ADD))
                ch.link(e.scalar_tensor_tensor(u, cv[:, 2:T + 2], tap(2), u, MUL, ADD))
                e.tensor_tensor(sc_y[:, pb, :], u, ps[:, 2 * pb + 1, 0:T], MUL).then_inc(free["sc_in"], 1)
                e.wait_ge(free["sc_in"], grp + (1 + CREDIT["sc_in"]))
                split(row(sc_hi, grp), row(sc_lo, grp), sc_y[:, pb, :], sc_ready)

            run("sc_in", sc_in_step, 10)

            def raw_copy(stage, sq_number, pair, bank, inc=None):
                e.wait_ge(sq_ready, sq_number + 1)
                ins = e.tensor_copy(flat(y[:, 2 * pair:2 * pair + 2, :]), ps[:, bank, :])
                ins.then_inc(inc, 1) if inc is not None else ch.mark(ins)

            run("sc_out", lambda it, b: raw_copy("sc_out", SQ["post"] + b, b, b))
            mods(2, 2)
            mods(3, 4)
            mods(4, 3)
            ch.mark(e.tensor_tensor(gain_post[:, :], mod[:, 16:24], pcol("gains", 8, 8), MUL))
            ch.link(e.scalar_tensor_tensor(gain_pre_ff[:, :], mod[:, 32:40], 1.0, pcol("gains", 16, 8), ADD, MUL))
            invert(STATN["post"], T)
            post_norm(gain_post)
            invert(STATN["pre_ff"], T)
            normalise("pre_ff", lambda i: gain_pre_ff[:, i:i + 1], 3)

            def mlp_in_step(it, b):
                e.wait_ge(hid_ready, it * 4 + (b + 1))
                pair = bass.ds(it * 8 + 2 * b, 2)
                split(hid_hi[:, pair, :], hid_lo[:, pair, :], hid[:, b % 2, :].rearrange("p (a c) -> p a c", a=2), hid_split)

            run("mlp_in", mlp_in_step, 4)
            for j in range(N_BLOCKS["mlp_out"]):
                ahead_at(FIRST["mlp_out"] + j + AHEAD)
                if j % 4 == 3:
                    t = j // 4
                    raw_copy("mlp_out", SQ["post_ff"] + t, t, t % 2, free["mlp_out"])
            mods(5, 5)
            ch.link(e.tensor_tensor(gain_post_ff[:, :], mod[:, 40:48], pcol("gains", 24, 8), MUL))
            e.wait_ge(free["mlp_out"], 4 + CREDIT["mlp_out"])
            invert(STATN["post_ff"], T)
            post_norm(gain_post_ff)
            invert(STATN["ln1"], T)
            normalise("ln1", lambda i: pcol("ln1", i), None)

            ch.link(e.tensor_scalar(qk_gain[:, 0:1], pcol("qk_g", 0), 0.125, None, MUL))

            def conv(lo_step, hi_step):
                for n in range(lo_step, min(hi_step, 4 * CV_TAPS)):
                    i, tap = 2 * (n // (2 * CV_TAPS)) + n % 2, n % (2 * CV_TAPS) // 2
                    src, wt = cpad[:, i, tap:tap + T], pcol("cv_w", CV_TAPS * i + tap)
                    if tap == 0:
                        e.wait_ge(c_in, i + 1)
                        e.wait_ge(wm_ready, 2)
                        e.tensor_scalar(cacc[:, i, :], src, wt, pcol("cv_b", i), MUL, ADD).then_inc(conv_step, 1)
                    else:
                        e.wait_ge(conv_step, n - 1)
                        e.scalar_tensor_tensor(cacc[:, i, :], src, wt, cacc[:, i, :], MUL, ADD).then_inc(conv_step, 1)

            def softplus(p):
                e.wait_ge(sp_log, p + 1)
                if p:
                    e.wait_ge(loga_done, p)
                zb = Z_BANKS[p % 2]
                e.scalar_tensor_tensor(sp[:, :, 0:384], ps[:, zb:zb + 2, 0:384], 0.0, sp_t[:, :, :], MAX, ADD)\
                 .then_inc(sp_ready, 1)

            def clamp(p):
                e.wait_ge(loga_done, p + 1)
                if p:
                    e.wait_ge(att_done, p)
                zb = Z_BANKS[p % 2]
                e.tensor_scalar(att[:, :, 0:384], ps[:, zb:zb + 2, 0:384], 0.0, None, ALU.min).then_inc(loga_low, 1)

            def att_out(p):
                e.wait_ge(att_done, p + 1)
                split(br["c"][0][:, p, :], br["c"][1][:, p, :], ps[:, MISC, T * (p % 2):T * (p % 2) + T], br_c)

            for s, kind in enumerate(Z_ORDER):
                g = FIRST["z_in"] + s
                ahead_at(g + AHEAD)
                bank = Z_FILL[s] % 2 if s in Z_FILL else None
                if kind in ("q", "k"):
                    raw_copy("z_in", SQ["qk"] + s, s, bank, z_free_dve)
                if 1 <= s <= 4:
                    t = s - 1
                    if t:
                        e.wait_ge(qk_ready, t)
                    invert(STATN["qk"] + t, 2 * T)
                    e.wait_ge(z_free_dve, t + 1)
                    gain = qk_gain[:, 0:1] if t < 2 else pcol("qk_g", 1)
                    pair = flat(y[:, 2 * t:2 * t + 2, :])
                    e.scalar_tensor_tensor(pair, pair, gain, rstd[:, :], MUL, MUL).then_inc(qk_ready, 1)
                if kind == "vv" and Z_ORDER[s + 1] != "vv":
                    e.wait_ge(w_used, g + 1 + USED)
                    for c in range(2):
                        e.tensor_copy(vv[:, c, :], ps[:, TOKEN_BANK + c, :]).then_inc(vv_ready, 1)
                if kind == "pg":
                    i = s - Z_ORDER.index("pg")
                    e.wait_ge(sig_ready, i + 1)
                    e.tensor_tensor(cpad[:, i, CV_TAPS - 1:], ps[:, bank, 0:T], sig[:, i % 2, :], MUL).then_inc(c_in, 1)
                if kind == "v" and Z_ORDER[s + 1] != "v":
                    for c in range(2):
                        e.wait_ge(vg_ready, c + 1)
                        ch.link(e.bn_stats(bn[:, c, 0:6], vg[:, c, :]))
                        e.bn_aggr(bn[:, c, 6:8], bn[:, c, 0:6]).then_inc(vg_var, 1)
                if s == VLN_STEP:
                    e.wait_ge(vg_std, 2)
                    e.wait_ge(wm_ready, 2)
                    ch.link(e.reciprocal(vstd[:, 2:4], vstd[:, 0:2]))
                    for c in range(2):
                        v = vg[:, c, :]
                        ch.link(e.tensor_scalar(v, v, bn[:, c, 6:7], vstd[:, 2 + c:3 + c], SUB, MUL))
                        ch.link(e.tensor_tensor(v, v, sgln[:, 0, :], MUL))
                        e.tensor_tensor(v, v, sgln[:, 1, :], ADD).then_inc(vln_ready, 1)
                if s == SG_STEP:
                    e.wait_ge(sg_done, 1)
                    e.wait_ge(z_free_act, 2)
                    for t in range(4):
                        o = sgo[:, t, :]
                        for c in range(2):
                            ch.mark(e.tensor_tensor(o[:, c * P:(c + 1) * P],
                                                    ps[:, SG_BANK + t // 2, T * (t % 2) + c * P:T * (t % 2) + (c + 1) * P],
                                                    sgb[:, t, :], ADD))
                        ch.wait()
                        ch.link(e.tensor_tensor(o, o, u_sb[:, t, :], MUL))
                        split(br["a"][0][:, t, :], br["a"][1][:, t, :], o, br_a)
                if s in CONV_STEPS:
                    k = s - CONV_STEPS[0]
                    conv(k * CONV_PER_STEP, (k + 1) * CONV_PER_STEP)
                for p in range(4):
                    if s == U_STEP(p):
                        clamp(p)
                for p in range(4):
                    if s == QK_STEP(p):
                        softplus(p)
                    if s == AV_STEP(p):
                        att_out(p)
                if s == CV_MEAN_STEP:
                    e.wait_ge(cv_mean, 1)
                    for i in range(4):
                        e.scalar_tensor_tensor(cacc[:, i, :], ps[:, STAT, 0:T], -1.0 / SG, cacc[:, i, :], MUL, ADD)\
                         .then_inc(cv_cent, 1)
                if s == CV_VAR_STEP:
                    invert(STATN["cv"], T)
                    for i in range(4):
                        e.scalar_tensor_tensor(cacc[:, i, :], cacc[:, i, :], pcol("cv_g", i), rstd[:, 0:T], MUL, MUL)\
                         .then_inc(cv_norm, 1)
                    for i in range(4):
                        e.wait_ge(cv_silu, i + 1)
                        split(br["b"][0][:, i, :], br["b"][1][:, i, :], cacc[:, i, :], br_b)

            for j in range(N_BLOCKS["branch"]):
                ahead_at(FIRST["branch"] + j + AHEAD)
                e.wait_ge(w_used, FIRST["branch"] + j + 1 + USED)
                e.wait_ge(gates_ready, 1 if j < 2 else 2)
                if j:
                    e.wait_ge(mix_ready, j)
                bk = 2 * (j % 2)
                ch.mark(e.tensor_tensor(flat(mg_t[:, 0:2, :]), ps[:, bk, :], flat(gates[:, 3 * j:3 * j + 2, :]), MUL))
                e.tensor_tensor(mg_t[:, 2, :], ps[:, bk + 1, 0:T], gates[:, 3 * j + 2, :], MUL).then_inc(free["branch"], 1)
                ch.wait()
                m = mg_t[:, 0, :]
                ch.link(e.tensor_tensor(m, m, mg_t[:, 1, :], ADD))
                e.wait_ge(free["branch"], j + 1 + CREDIT["branch"])
                ch.link(e.tensor_tensor(m, m, mg_t[:, 2, :], ADD))
                split(a_hi[:, j, :], a_lo[:, j, :], m, mix_ready)
            for j in range(N_BLOCKS["mix_out"]):
                ahead_at(FIRST["mix_out"] + j + AHEAD)
                e.wait_ge(w_used, FIRST["mix_out"] + j + 1 + USED)
                pair = flat(x[:, 2 * j:2 * j + 2, :])
                e.tensor_tensor(pair, pair, ps[:, j, :], ADD).then_inc(x_new, 2)
            e.wait_ge(x_new, X_NEW["ln2"] + DT)
            invert(STATN["ln2"], T)
            normalise("ln2", lambda i: pcol("ln2", i), None)

            def product(it, b):
                e.wait_ge(up_g_ready, it * 4 + (b + 1))
                ch.link(e.tensor_tensor(up_p[:, b % 2, :], up_g[:, b % 2, :], up_u[:, b % 2, T:2 * T], MUL))
                i = it * 4 + b
                split(row(up_hi, i), row(up_lo, i), up_p[:, b % 2, :], up_ready)

            def up_step(it, b):
                e.wait_ge(up_u_ready, it * 8 + (2 * b + 2))
                for tap in (1, 0):
                    for h in range(2):
                        o = 2 - tap
                        dst = up_u[:, b % 2, h * T + o:(h + 1) * T]
                        ins = e.scalar_tensor_tensor(dst, ps[:, b, h * T:(h + 1) * T - o],
                                                     pdyn("up_w", it * 24 + (3 * (2 * b + h) + tap)), dst, MUL, ADD)
                        if tap == 0 and h == 1:
                            ins.then_inc(free["up"], 1)
                        else:
                            ch.mark(ins)
                    if tap == 1:
                        ch.wait()
                if isinstance(it, int):
                    if 4 * it + b >= 1:
                        product((4 * it + b - 1) // 4, (b - 1) % 4)
                else:
                    product(it - 1, 3) if b == 0 else product(it, b - 1)

            run("up", up_step, 4 * 5)
            product(5, 1)
            for j in range(N_BLOCKS["down"]):
                ahead_at(FIRST["down"] + j + AHEAD)
                if j % 4 == 3:
                    t = j // 4
                    e.wait_ge(w_used, FIRST["down"] + j + 1 + USED)
                    pair = flat(x[:, 2 * t:2 * t + 2, :])
                    e.tensor_tensor(pair, pair, ps[:, 2 + t % 2, :], ADD).then_inc(out_ready, 1)

        @block.tensor
        def _(pe):
            e = pe

            def product(dst, slot, tile, hi, lo, start, stop):
                cols = slice(tile * P, (tile + 1) * P)
                e.matmul(dst, w_hi[:, slot, cols], hi, start=start, stop=False)
                e.matmul(dst, w_hi[:, slot, cols], lo, start=False, stop=False)
                return e.matmul(dst, w_lo[:, slot, cols], hi, start=False, stop=stop)

            def half(bank, h):
                return ps[:, bank, h * T:(h + 1) * T]

            def sum_squares(number, stat, first, last):
                e.wait_ge(sq_ready, number + 1)
                if first and stat:
                    e.wait_ge(std_ready, stat)
                for h in range(2):
                    mm = e.matmul(ps[:, STAT, 0:T], ones[:, :], sq[:, number % 2, h * T:(h + 1) * T],
                                  start=first and h == 0, stop=last and h == 1)
                mm.then_inc(sq_used, 1)

            def mod_sums(vector, acc):
                for i in range(DT):
                    n = DT * vector + i
                    mm = e.matmul(ps[:, MISC, n:n + 1], acc[:, i * P:(i + 1) * P], ones[:, 0:1],
                                  start=True, stop=True)
                mm.then_inc(mod_ps, 1)

            e.wait_ge(const_set, 2)
            for t in range(4):
                sum_squares(SQ["x"] + t, STATN["x"], t == 0, t == 3)
            e.wait_ge(raw_used, 4)
            mod_sums(1, ada_acc[:, 1, :])
            e.wait_ge(raw_used, ADA_FIRST)
            e.wait_ge(mod_read, 1)
            mod_sums(0, ada_acc[:, 0, :])

            e.wait_ge(act_lo, ACT_TILE["x"] + DT)
            g0 = FIRST["sc_in"]
            with e.Fori(0, N_BLOCKS["sc_in"] // 4) as it:
                for b in range(4):
                    if b % 2 == 0:
                        e.wait_ge(free["sc_in"], it * 2 + (b // 2 + 1))
                    e.wait_ge(raw_used, it * 8 + (raw_unit(g0 + b) + 1))
                    for t in range(12):
                        n, k = divmod(12 * (b % 2) + t, DT)
                        dst = half(2 * (b // 2) + n // 2, n % 2)
                        mm = product(dst, (g0 + b) % SPLIT_SLOTS, t, a_hi[:, k, :], a_lo[:, k, :], k == 0, k == DT - 1)
                    mm.then_inc(w_used, 1)

            def pair_block(g, static_g, banks, hi, lo):
                e.wait_ge(raw_used, g)
                for t in range(16):
                    n, k = divmod(t, DT)
                    mm = product(half(banks, n), static_g % SPLIT_SLOTS, t, hi[:, k, :], lo[:, k, :], k == 0, k == DT - 1)
                mm.then_inc(w_used, 1)

            e.wait_ge(sc_ready, DT)
            g0 = FIRST["sc_out"]
            for j in range(4):
                pair_block(raw_unit(g0 + j) + 1, g0 + j, j, sc_hi, sc_lo)
                if j == 3:
                    e.wait_ge(mod_read, 2)
                    e.wait_ge(raw_used, raw_unit(g0 + 4))
                    for n, vector in enumerate((2, 4, 3)):
                        mod_sums(vector, ada_acc[:, 2 + n, :])
                if j >= 1:
                    sum_squares(SQ["post"] + j - 1, STATN["post"], j == 1, False)
            sum_squares(SQ["post"] + 3, STATN["post"], False, True)

            def x_norm(norm):
                for t in range(4):
                    sum_squares(SQ[norm] + t, STATN[norm], t == 0, t == 3)
                e.wait_ge(act_lo, ACT_TILE[norm] + DT)

            x_norm("pre_ff")
            g0 = FIRST["mlp_in"]
            with e.Fori(0, N_BLOCKS["mlp_in"] // 4) as it:
                for b in range(4):
                    e.wait_ge(free["mlp_in"], it * 4 + (b + 1))
                    pair_block(it * 4 + (raw_unit(g0 + b) + 1), g0 + b, b, a_hi, a_lo)

            g0 = FIRST["mlp_out"]
            for j in range(16):
                t, n, k0 = j // 4, j % 4 // 2, 16 * (j % 2)
                if j % 4 == 0:
                    e.wait_ge(free["mlp_out"], t + 1)
                if j < 2:
                    e.wait_ge(hid_split, 13 if j == 0 else 16)
                e.wait_ge(raw_used, raw_unit(g0 + j) + 1)
                for k in range(k0, k0 + 16):
                    mm = product(half(t % 2, n), (g0 + j) % SPLIT_SLOTS, k - k0, hid_hi[:, k, :], hid_lo[:, k, :],
                                 k == 0, k == 31)
                mm.then_inc(w_used, 1)
                if j == 10:
                    e.wait_ge(raw_used, raw_unit(44))
                    mod_sums(5, hid[:, :, :].rearrange("p a b -> p (a b)"))
                if j % 4 == 1 and t:
                    sum_squares(SQ["post_ff"] + t - 1, STATN["post_ff"], t == 1, False)
            sum_squares(SQ["post_ff"] + 3, STATN["post_ff"], False, True)
            x_norm("ln1")

            e.wait_ge(const_set, N_CONST)
            g0 = FIRST["z_in"]

            def token_block(j, k0):
                e.wait_ge(raw_used, raw_unit(g0 + j) + 1)
                slot = (g0 + j) % SPLIT_SLOTS
                for c in range(2):
                    dst, tok = ps[:, TOKEN_BANK + c, :], slice(c * P, (c + 1) * P)
                    for k in range(k0, k0 + 4):
                        cols = slice((k - k0) * SG, (k - k0 + 1) * SG)
                        e.matmul(dst, a_hi[:, k, tok], w_hi[:, slot, cols], start=k == 0, stop=False)
                        e.matmul(dst, a_hi[:, k, tok], w_lo[:, slot, cols], start=False, stop=False)
                        mm = e.matmul(dst, a_lo[:, k, tok], w_hi[:, slot, cols], start=False, stop=k == DT - 1)
                mm.then_inc(w_used, 1)

            def scores(p):
                zb = Z_BANKS[p % 2]
                e.wait_ge(qk_ready, 4)
                e.wait_ge(vg_ready, 2)
                if p == 1:
                    e.wait_ge(br_a, 4)
                if p >= 2:
                    e.wait_ge(att_exp, p - 1)
                for h in range(2):
                    f = slice(64 * h, 64 * h + 64)
                    e.matmul(ps[:, zb + h, 0:T], y[f, 4 + p, 0:P], y[f, p, :], start=True, stop=True,
                             skip_group_check=True)
                    mm = e.matmul(ps[:, zb + h, T:T + P], y[f, 4 + p, P:T], y[f, p, P:T], start=False, stop=True,
                                  skip_group_check=True)
                mm.then_inc(z_done, 1)

            def log_weights(p):
                zb = Z_BANKS[p % 2]
                e.wait_ge(sp_masked, p + 1)
                for h in range(2):
                    e.matmul(ps[:, zb + h, 0:T], neg_upper[:, :], sp[:, h, 0:T], start=False, stop=True,
                             skip_group_check=True)
                    e.matmul(ps[:, zb + h, P:T], neg_ones[:, :], sp[:, h, T:T + P], start=False, stop=True,
                             skip_group_check=True)
                    mm = e.matmul(ps[:, zb + h, T:T + P], neg_upper[:, :], sp[:, h, T:T + P], start=False, stop=True,
                                  skip_group_check=True)
                mm.then_inc(loga_done, 1)

            def att_values(p):
                e.wait_ge(att_ready, p + 1)
                if p == 0:
                    e.wait_ge(vv_ready, 2)
                if p >= 2:
                    e.wait_ge(br_c, p - 1)
                c0 = T * (p % 2)
                for h in range(2):
                    f = slice(64 * h, 64 * h + 64)
                    cols = slice(64 * (2 * p + h), 64 * (2 * p + h + 1))
                    e.matmul(ps[f, MISC, c0:c0 + T], vv[:, 0, cols], att[:, h, 0:T], start=True, stop=True)
                    mm = e.matmul(ps[f, MISC, c0 + P:c0 + T], vv[:, 1, cols], att[:, h, T:T + P], start=False, stop=True,
                                  skip_group_check=True)
                mm.then_inc(att_done, 1)

            def spatial_gating():
                e.wait_ge(vln_ready, 2)
                e.wait_ge(wm_ready, 2)
                for t in range(4):
                    for c in range(2):
                        for h in range(2):
                            grp = 2 * t + h
                            mm = e.matmul(ps[64 * h:64 * h + 64, SG_BANK + t // 2, T * (t % 2) + c * P:T * (t % 2) + (c + 1) * P],
                                          vg[:, c, 64 * grp:64 * grp + 64], wm[:, grp, :], start=True, stop=True,
                                          skip_group_check=True)
                mm.then_inc(sg_done, 1)

            for s, kind in enumerate(Z_ORDER):
                if kind in ("v", "vv"):
                    first = Z_ORDER[s - 1] != kind
                    if kind == "v" and first:
                        e.wait_ge(vv_ready, 2)
                    token_block(s, 0 if first else 4)
                else:
                    f = Z_FILL[s]
                    if 2 <= f < 6:
                        e.wait_ge(z_free_dve, f - 1)
                    elif 6 <= f < 10:
                        e.wait_ge(c_in, f - 5)
                    elif f >= 10:
                        e.wait_ge(z_free_act, f - 9)
                    pair_block(raw_unit(g0 + s) + 1, g0 + s, f % 2, a_hi, a_lo)
                if 1 <= s <= 4:
                    t = s - 1
                    e.wait_ge(sq_ready, SQ["qk"] + t + 1)
                    e.wait_ge(std_ready, STATN["qk"] + t)
                    e.matmul(ps[:, STAT, :], head_ones[:, :], sq[:, (SQ["qk"] + t) % 2, :], start=True, stop=True)\
                     .then_inc(sq_used, 1)
                if s == SG_STEP:
                    spatial_gating()
                for p in range(4):
                    if s == U_STEP(p):
                        log_weights(p)
                for p in range(4):
                    if s == QK_STEP(p):
                        scores(p)
                for p in range(4):
                    if s == AV_STEP(p):
                        att_values(p)
                if s == CV_MEAN_STEP:
                    e.wait_ge(conv_step, 4 * CV_TAPS)
                    e.wait_ge(std_ready, STATN["cv"])
                    for i in range(4):
                        mm = e.matmul(ps[:, STAT, 0:T], ones[:, :], cacc[:, i, :], start=i == 0, stop=i == 3)
                    mm.then_inc(cv_mean, 1)
                if s == CV_VAR_STEP:
                    e.wait_ge(cv_cent, 4)
                    for t in range(2):
                        sum_squares(SQ["cv"] + t, 0, t == 0, t == 1)

            e.wait_ge(z_free_act, 14)
            g0 = FIRST["branch"]
            with e.Fori(0, N_BLOCKS["branch"] // 4) as it:
                for b in range(4):
                    e.wait_ge(free["branch"], it * 4 + (b + 1))
                    e.wait_ge(raw_used, it * 4 + (raw_unit(g0 + b) + 1))
                    for n, (name, ready) in enumerate((("a", br_a), ("b", br_b), ("c", br_c))):
                        e.wait_ge(ready, 4)
                        for k in range(4):
                            mm = product(half(2 * (b % 2) + n // 2, n % 2), (g0 + b) % SPLIT_SLOTS, 4 * n + k,
                                         br[name][0][:, k, :], br[name][1][:, k, :], k == 0, k == 3)
                    mm.then_inc(w_used, 1)

            e.wait_ge(mix_ready, DT)
            g0 = FIRST["mix_out"]
            with e.Fori(0, 1) as it:
                for j in range(4):
                    pair_block(raw_unit(g0 + j) + 1, g0 + j, j, a_hi, a_lo)
            x_norm("ln2")

            g0 = FIRST["up"]
            n = N_BLOCKS["up"]
            with e.Fori(0, n // 4) as it:
                for b in range(4):
                    e.wait_ge(free["up"], it * 4 + (b + 1))
                    pair_block(it * 4 + (raw_unit(g0 + b) + 1), g0 + b, b, a_hi, a_lo)
            for j in range(n // 4 * 4, n):
                e.wait_ge(free["up"], j + 1)
                pair_block(raw_unit(g0 + j) + 1, g0 + j, j % 4, a_hi, a_lo)

            g0 = FIRST["down"]
            for j in range(16):
                t, n, k0 = j // 4, j % 4 // 2, 11 * (j % 2)
                if j % 4 == 0 and t >= 2:
                    e.wait_ge(out_ready, t - 1)
                if j < 2:
                    e.wait_ge(up_ready, 20 if j == 0 else 22)
                e.wait_ge(raw_used, raw_unit(g0 + j) + 1)
                for k in range(k0, k0 + 11):
                    mm = product(half(2 + t % 2, n), (g0 + j) % SPLIT_SLOTS, k - k0, up_hi[:, k, :], up_lo[:, k, :],
                                 k == 0, k == 21)
                mm.then_inc(w_used, 1)


def _stationary(weight, order, per_block):
    import numpy as np
    k, n = weight.shape
    t = weight.reshape(k // P, P, n // P, P).transpose(2, 0, 1, 3)[np.array(order)]
    return np.ascontiguousarray(t.reshape(-1, per_block, P, P).transpose(0, 2, 1, 3).reshape(-1, P, per_block * P))


def _columns(vector):
    return vector.reshape(-1, P).T


def kernel(**inputs):
    import numpy as np
    import concourse.bacc as bacc
    from concourse.bass_utils import run_bass_kernel_spmd

    a = {name: np.asarray(value) for name, value in inputs.items()}
    per = {name: t for name, _, t in STAGES}
    w = {}
    w["sc_in"] = _stationary(a["sc_w_in"][0], [g + i for i in range(DT) for g in (8, 16, 0)], per["sc_in"])
    w["sc_out"] = _stationary(a["sc_w_out"][0], range(8), per["sc_out"])
    w["mlp_in"] = _stationary(a["mlp_w_in"][0], range(32), per["mlp_in"])
    w["mlp_out"] = _stationary(a["mlp_w_out"][0], range(8), per["mlp_out"])
    w_z = a["w_in_2"][0]

    def token_major(first_col):
        t = w_z[:, first_col:first_col + SG].reshape(2, 4, P, SG)
        return t.transpose(0, 2, 1, 3).reshape(2, P, 4 * SG)

    z_tiles = lambda order: _stationary(w_z, order, per["z_in"])
    w["z_in"] = np.concatenate([
        z_tiles(range(16, 24)),
        token_major(3072),
        z_tiles([t + i for i in range(4) for t in (8, 12)]),
        token_major(512),
        z_tiles(range(0, 4)),
        z_tiles([28 + 8 * br + i for i in range(DT) for br in range(3)]),
    ])
    br = [a[name][0].reshape(4, P, DT, P).transpose(2, 0, 1, 3) for name in ("w_a_out_2", "w_b_out_2", "w_c_out_2")]
    w["branch"] = np.ascontiguousarray(np.stack(br, 1).reshape(DT, 12, P, P).transpose(0, 2, 1, 3).reshape(DT, P, 12 * P))
    w["mix_out"] = _stationary(a["w_out_2"][0], range(8), per["mix_out"])
    gate_value = [t + i for i in range(22) for t in (0, 22)]
    w["up"] = _stationary(a["w_up_2"][0], gate_value, per["up"])
    w["down"] = _stationary(a["w_down_2"][0], range(8), per["down"])

    ada = a["ada_w"][0].reshape(DT, P, 6, D).transpose(2, 0, 1, 3)
    ada_half = ada[[2, 4]].transpose(1, 0, 2, 3).reshape(16, P, D)
    ada = ada[[1, 0, 3, 5]].reshape(16, 2, P, D).transpose(0, 2, 1, 3).reshape(16, P, UNIT)

    taps = lambda t: t.T.reshape(-1, P, t.shape[0]).transpose(1, 0, 2)
    parts = {
        "c": _columns(a["c"][0]), "ada_b": _columns(a["ada_b"][0]), "gains": _columns(a["norm_gains"][0]),
        "sc_conv": taps(a["sc_conv"][0]), "ln1": _columns(a["ln1_g_2"][0]),
        "b_gate": a["b_gate_2"][0].reshape(3, DT, P).transpose(2, 1, 0),
        "cv_w": taps(a["cv_w_2"][0]), "cv_b": _columns(a["cv_b_2"][0]), "cv_g": _columns(a["cv_ln_g_2"][0]),
        "cv_lb": _columns(a["cv_ln_b_2"][0]),
        "qk_g": np.stack([np.tile(a["q_norm_g_2"][0], 2), np.tile(a["k_norm_g_2"][0], 2)], 1),
        "ln2": _columns(a["ln2_g_2"][0]),
        "up_w": taps(a["ffn_conv_w_2"][0])[:, gate_value], "up_b": _columns(a["ffn_conv_b_2"][0])[:, gate_value],
    }
    params = np.concatenate([parts[name].reshape(P, n) for name, n in PARAMS], 1)
    arrays = {
        "x": a["x"][0].T.reshape(DT, P, T).transpose(1, 0, 2), "params": params, "ada": ada, "ada_half": ada_half,
        **{"w_" + name: value for name, value in w.items()},
        "wm_t": a["sg_w_2"][0].transpose(2, 0, 1),
        "sg_bias": np.repeat(a["sg_b_2"][0].reshape(4, 2, 1, P), 64, axis=2).reshape(4, P, P).transpose(1, 0, 2),
        "sg_ln": np.broadcast_to(np.stack([a["sg_ln_g_2"][0], a["sg_ln_b_2"][0]]), (P, 2, SG)),
    }
    arrays = {name: np.ascontiguousarray(value) for name, value in arrays.items()}
    nc = bacc.Bacc("TRN2", target_bir_lowering=False, num_devices=1)
    f32 = mybir.dt.float32
    ap = {name: nc.dram_tensor("in_" + name, value.shape, f32, kind="ExternalInput").ap() for name, value in arrays.items()}
    out = nc.dram_tensor("out", (P, DT, T), f32, kind="ExternalOutput").ap()
    build_program(nc, ap["x"], ap["params"], ap["ada"], ap["ada_half"], {name: ap["w_" + name] for name in w}, ap["wm_t"], ap["sg_bias"],
          ap["sg_ln"], out)
    r = run_bass_kernel_spmd(nc, [{"in_" + name: value for name, value in arrays.items()}], core_ids=[0])
    return r.results[0]["out"].transpose(1, 0, 2).reshape(D, T).T.reshape(1, T, D)
```

```python
import concourse.bass as bass
from concourse import mybir
from contextlib import ExitStack, contextmanager

P = 128
T = 256
D = 1024
DT = D // P
RAW_SLOTS = 4
SPLIT_SLOTS = 4
AHEAD = SPLIT_SLOTS - 1
UNIT = 2048
EPS = 1e-6
SG = 512
CV_TAPS = 31
HEADS = 8

STAGES = [("sc_in", 16, 12), ("sc_out", 4, 16), ("mlp_in", 16, 16), ("mlp_out", 16, 16),
          ("z_in", 26, 16), ("branch", 8, 12), ("mix_out", 4, 16), ("up", 22, 16), ("down", 16, 11)]
N_BLOCKS = {name: n for name, n, _ in STAGES}
WORDS = {name: t * P for name, _, t in STAGES}
FIRST = {}
STAGE_OF = []
for _name, _n, _ in STAGES:
    FIRST[_name] = len(STAGE_OF)
    STAGE_OF += [_name] * _n
ADA_FIRST = 8
ADA_AFTER = {"sc_in": range(0, 16), "sc_out": range(17, 21), "mlp_out": range(40, 44)}
CREDIT = {"sc_in": 2, "mlp_in": 4, "mlp_out": 2, "branch": 2, "up": 4}
Z_ORDER = ["pg"] * 4 + ["q", "q", "k", "k", "vv", "vv"] + ["v", "v", "u", "u"] + ["gate"] * 12
QK_FIRST = Z_ORDER.index("q")
PARAMS = [("c", 8), ("ada_b", 48), ("gains", 32), ("sc_conv", 24), ("ln1", 8), ("b_gate", 24),
          ("cv_w", 4 * CV_TAPS), ("cv_b", 4), ("cv_g", 4), ("cv_lb", 4), ("qk_g", 2), ("ln2", 8),
          ("up_w", 132), ("up_b", 44)]
PCOL = {}
_at = 0
for _name, _n in PARAMS:
    PCOL[_name] = _at
    _at += _n
N_PARAMS = _at
N_CONST = 10
Z_FILL = {s: n for n, s in enumerate(s for s, kind in enumerate(Z_ORDER) if kind not in ("v", "vv"))}
VLN_STEP, SG_STEP = 13, 14
QK_STEP = lambda p: 13 + 2 * p
U_STEP = lambda p: 15 + 2 * p
AV_STEP = lambda p: 17 + 2 * p
CONV_AT = {**{s: 7 for s in range(2, 8)}, **{s: 8 for s in range(8, 13)}, 13: 4, 14: 2, **{s: 6 for s in range(15, 21)}}
CV_MEAN_STEP, CV_VAR_STEP = 21, 22


def raw_unit(block):
    return ADA_FIRST + block + sum(min(max(block - r.start, 0), len(r)) for r in ADA_AFTER.values())


def has_ada(block):
    return any(block in r for r in ADA_AFTER.values())


class Chain:

    def __init__(self, eng, sem):
        self.eng, self.sem, self.n, self.base = eng, sem, 0, 0

    def mark(self, ins):
        ins.then_inc(self.sem, 1)
        self.n += 1
        return self.n

    def wait(self, n=None):
        self.eng.wait_ge(self.sem, self.base + (self.n if n is None else n))

    def link(self, ins):
        self.mark(ins)
        self.wait()

    @contextmanager
    def loop(self, first, end, per):
        start = self.n
        with self.eng.Fori(first, end) as it:
            self.base = it * per - first * per
            yield it
        assert self.n == start + per, self.n - start
        self.n, self.base = start + (end - first) * per, 0


def build_program(nc, x_in, params, ada, ada_half, w, wm_t, sg_bias, sg_ln, out):
    f32, f32r = mybir.dt.float32, mybir.dt.float32r
    ALU, ACT = mybir.AluOpType, mybir.ActivationFunctionType
    ADD, SUB, MUL, MAX = ALU.add, ALU.subtract, ALU.mult, ALU.max
    ctx = ExitStack()
    with ctx:
        def sb(name, shape, dt=f32, c=ctx):
            return c.enter_context(nc.sbuf_tensor(name, shape, dt))

        def sem(name):
            return ctx.enter_context(nc.semaphore(name))

        raw = sb("raw", [P, RAW_SLOTS, UNIT])
        w_hi = sb("w_hi", [P, SPLIT_SLOTS, UNIT], f32r)
        w_lo = sb("w_lo", [P, SPLIT_SLOTS, UNIT], f32r)
        par = sb("par", [P, N_PARAMS])
        x = sb("x", [P, DT, T])
        a_hi = sb("a_hi", [P, DT, T], f32r)
        a_lo = sb("a_lo", [P, DT, T], f32r)
        y = sb("y", [P, DT, T])
        sq = sb("sq", [P, 2, 2 * T])
        rstd = sb("rstd", [P, 2, 2 * T])
        mod = sb("mod", [P, 48])
        silu_c = sb("silu_c", [P, DT])
        gain_pre = sb("gain_pre", [P, DT])
        gain_post = sb("gain_post", [P, DT])
        gain_pre_ff = sb("gain_pre_ff", [P, DT])
        gain_post_ff = sb("gain_post_ff", [P, DT])
        qk_gain = sb("qk_gain", [P, 2])
        eps = sb("eps", [P, 1])
        ones = sb("ones", [P, P])

        with ExitStack() as c:
            ada_acc = sb("ada_acc", [P, 5, D], c=c)
            sc_hi = sb("sc_hi", [P, DT, T], f32r, c=c)
            sc_lo = sb("sc_lo", [P, DT, T], f32r, c=c)
            sc_c = sb("sc_c", [P, 2, T], c=c)
            sc_cv = sb("sc_cv", [P, 2, T + 2], c=c)
            sc_u = sb("sc_u", [P, 2, T], c=c)
            sc_y = sb("sc_y", [P, 2, T], c=c)
        with ExitStack() as c:
            hid_hi = sb("hid_hi", [P, 32, T], f32r, c=c)
            hid_lo = sb("hid_lo", [P, 32, T], f32r, c=c)
            hid = sb("hid", [P, 2, 2 * T], c=c)
        with ExitStack() as c:
            br = {}
            for name in ("a", "c"):
                br[name] = [sb(f"br_{name}_{part}", [P, 4, T], f32r, c=c) for part in ("hi", "lo")]
            cacc = sb("cacc", [P, 4, T], c=c)
            vv = sb("vv", [P, 2, SG], c=c)
            head_ones = sb("head_ones", [P, P], c=c)
            neg_upper = sb("neg_upper", [P, P], c=c)
            neg_ones = sb("neg_ones", [P, P], c=c)
            bn = sb("bn", [P, 2, 8], c=c)
            vstd = sb("vstd", [P, 4], c=c)
            with ExitStack() as early:
                sig = sb("sig", [P, 2, T], c=early)
                sb("unused_gates_head", [P, 4, T], c=early)
                sgo = sb("sgo", [P, 4, T], c=early)
                vg = sb("vg", [P, 2, SG], c=early)
                wm = sb("wm", [P, HEADS, P], c=early)
                sgb = sb("sgb", [P, 4, P], c=early)
                sgln = sb("sgln", [P, 2, SG], c=early)
            gates = sb("gates", [P, 24, T], c=c)
            with ExitStack() as early:
                cpad = sb("cpad", [P, 4, T + CV_TAPS - 1], c=early)
                sp_t = sb("sp_t", [P, 2, 384], c=early)
            br["b"] = [sb(f"br_b_{part}", [P, 4, T], f32r, c=c) for part in ("hi", "lo")]
            with ExitStack() as late:
                mg_t = sb("mg_t", [P, 3, T], c=late)
            sp = sb("sp", [P, 2, 512], c=c)
            with ExitStack() as early:
                u_sb = sb("u_sb", [P, 4, T], c=early)
            att = sb("att", [P, 2, 512], c=c)
        with ExitStack() as c:
            up_hi = sb("up_hi", [P, 22, T], f32r, c=c)
            up_lo = sb("up_lo", [P, 22, T], f32r, c=c)
            up_u = sb("up_u", [P, 2, 2 * T], c=c)
            up_g = sb("up_g", [P, 2, T], c=c)
            up_p = sb("up_p", [P, 2, T], c=c)

        ps = ctx.enter_context(nc.psum_tensor("ps", [P, 8, 2 * T], f32))
        STAT, MISC = 4, 5
        TOKEN_BANK = 2
        SG_BANK = 6
        Z_BANKS = [2, 6]

        raw_in = [sem(f"raw_in{i}") for i in range(RAW_SLOTS)]
        raw_used = sem("raw_used")
        w_high = sem("w_high")
        w_used = sem("w_used")
        free = {s: sem(f"free_{s}") for s in CREDIT}
        par_in = sem("par_in")
        x_landed = sem("x_landed")
        z_const_in = sem("z_const_in")
        const_set = sem("const_set")
        c_ready = sem("c_ready")
        mod_ps = sem("mod_ps")
        mod_read = sem("mod_read")
        sq_ready = sem("sq_ready")
        sq_used = sem("sq_used")
        rstd_ready = sem("rstd_ready")
        norm_t = sem("norm_t")
        act_hi = sem("act_hi")
        act_lo = sem("act_lo")
        x_new = sem("x_new")
        sc_c_ready = sem("sc_c_ready")
        sc_cv_ready = sem("sc_cv_ready")
        sc_u_ready = sem("sc_u_ready")
        sc_hi_ready = sem("sc_hi_ready")
        sc_ready = sem("sc_ready")
        hid_ready = sem("hid_ready")
        hid_split = sem("hid_split")
        qk_raw = sem("qk_raw")
        z_free_act = sem("z_free_act")
        qk_ready = sem("qk_ready")
        vv_ready = sem("vv_ready")
        sig_ready = sem("sig_ready")
        c_in = sem("c_in")
        conv_step = sem("conv_step")
        vg_ready = sem("vg_ready")
        vg_var = sem("vg_var")
        vg_std = sem("vg_std")
        vln_ready = sem("vln_ready")
        wm_ready = sem("wm_ready")
        sg_done = sem("sg_done")
        br_a = sem("br_a")
        br_b = sem("br_b")
        br_c = sem("br_c")
        z_done = sem("z_done")
        sp_log = sem("sp_log")
        sp_ready = sem("sp_ready")
        sp_masked = sem("sp_masked")
        loga_done = sem("loga_done")
        loga_low = sem("loga_low")
        att_exp = sem("att_exp")
        att_ready = sem("att_ready")
        att_done = sem("att_done")
        cv_mean = sem("cv_mean")
        cv_cent = sem("cv_cent")
        cv_norm = sem("cv_norm")
        cv_silu = sem("cv_silu")
        gates_ready = sem("gates_ready")
        mix_sum = sem("mix_sum")
        mix_hi = sem("mix_hi")
        mix_ready = sem("mix_ready")
        up_u_ready = sem("up_u_ready")
        up_g_ready = sem("up_g_ready")
        up_ready = sem("up_ready")
        act_self = sem("act_self")
        dve_self = sem("dve_self")
        out_ready = sem("out_ready")
        out_sem = sem("out_sem")

        def pcol(name, i=0, n=1):
            return par[:, PCOL[name] + i:PCOL[name] + i + n]

        def pdyn(name, i):
            return pcol(name, i) if isinstance(i, int) else par[:, bass.ds(i + PCOL[name], 1)]

        def row(t, i):
            return t[:, i, :]

        def landed_at(unit):
            return 16 * (unit // RAW_SLOTS + 1)

        def flat(t):
            return t.rearrange("p a b -> p (a b)")

        SQ = {"x": 0, "post": 4, "pre_ff": 8, "post_ff": 12, "ln1": 16, "qk": 20, "cv": 24, "ln2": 26}
        STATN = {"x": 0, "post": 1, "pre_ff": 2, "post_ff": 3, "ln1": 4, "qk": 5, "cv": 9, "ln2": 10}
        ACT_TILE = {"x": 0, "pre_ff": 8, "ln1": 16, "ln2": 24}
        X_NEW = {"pre_ff": 0, "ln1": 8, "ln2": 16}
        USED = SPLIT_SLOTS

        block = ctx.enter_context(nc.Block())

        @block.sync
        def _(sp_eng):
            e = sp_eng
            e.dma_start(par[:, :], params[:, :]).then_inc(par_in, 16)

            def load(unit_wait, slot, words, src):
                if unit_wait is not None:
                    e.wait_ge(raw_used, unit_wait)
                e.dma_start(raw[:, slot, 0:words], src).then_inc(raw_in[slot], 16)

            for i in range(ADA_FIRST):
                load(i - RAW_SLOTS + 1 if i >= RAW_SLOTS else None, i % RAW_SLOTS, UNIT, ada[i])
                if i == 0:
                    e.dma_start(x[:, :, :], x_in).then_inc(x_landed, 16)
            ada_next = ADA_FIRST
            for s, n, _ in STAGES:
                u0 = raw_unit(FIRST[s])
                if s == "sc_in":
                    with e.Fori(0, n // 4) as it:
                        for b in range(4):
                            u = u0 + 2 * b
                            load(it * 8 + (u - RAW_SLOTS + 1), u % RAW_SLOTS, WORDS[s], w[s][it * 4 + b])
                            load(it * 8 + (u - RAW_SLOTS + 2), (u + 1) % RAW_SLOTS, D, ada_half[it * 4 + b])
                    continue
                peeled = {"sc_out": n, "mlp_in": 4, "mlp_out": n}.get(s, 0)
                for j in range(peeled):
                    u = raw_unit(FIRST[s] + j)
                    load(u - RAW_SLOTS + 1, u % RAW_SLOTS, WORDS[s], w[s][j])
                    if has_ada(FIRST[s] + j):
                        load(u - RAW_SLOTS + 2, (u + 1) % RAW_SLOTS, UNIT, ada[ada_next])
                        ada_next += 1
                if peeled < n:
                    u0 = raw_unit(FIRST[s] + peeled) - peeled
                    with e.Fori(peeled // 4, n // 4) as it:
                        for b in range(4):
                            load(it * 4 + (u0 + b - RAW_SLOTS + 1), (u0 + b) % RAW_SLOTS, WORDS[s], w[s][it * 4 + b])
                    for j in range(n // 4 * 4, n):
                        load(u0 + j - RAW_SLOTS + 1, (u0 + j) % RAW_SLOTS, WORDS[s], w[s][j])
            for t in range(4):
                e.wait_ge(out_ready, t + 1)
                e.dma_start(out[:, 2 * t:2 * t + 2, :], x[:, 2 * t:2 * t + 2, :]).then_inc(out_sem, 16)
            e.wait_ge(out_sem, 64)

        @block.gpsimd
        def _(pool):
            e = pool
            e.sem_inc(w_used, USED)
            for s, n in CREDIT.items():
                e.sem_inc(free[s], n)
            def constant(ins, n):
                ins.then_inc(const_set, 1)
                e.wait_ge(const_set, n)

            constant(e.memset(eps[:, :], EPS), 1)
            constant(e.memset(ones[:, :], 1.0), 2)
            constant(e.memset(flat(ada_acc[:, 2:4, :]), 0.0), 3)
            constant(e.memset(sc_cv[:, :, :], 0.0), 4)
            e.wait_ge(w_used, USED + FIRST["z_in"])
            e.dma_start(wm[:, :, :], wm_t).then_inc(z_const_in, 16)
            e.dma_start(sgb[:, :, :], sg_bias).then_inc(z_const_in, 16)
            e.dma_start(sgln[:, :, :], sg_ln).then_inc(z_const_in, 16)
            constant(e.memset(head_ones[:, :], 0.0), 5)
            constant(e.memset(head_ones[0:64, 0:64], 1.0), 6)
            constant(e.memset(head_ones[64:128, 64:128], 1.0), 7)
            constant(e.memset(neg_ones[:, :], -1.0), 8)
            constant(e.memset(neg_upper[:, :], -1.0), 9)
            constant(e.affine_select(out=neg_upper[:, :], in_=neg_upper[:, :], pattern=[[-1, P]],
                                     compare_op=ALU.is_ge, fill=0.0, base=0, channel_multiplier=1), 10)
            e.wait_ge(z_const_in, 48)
            e.memset(cpad[:, :, 0:CV_TAPS - 1], 0.0).then_inc(wm_ready, 1)
            e.wait_ge(wm_ready, 1)
            e.affine_select(out=wm[:, :, :], in_=wm[:, :, :], pattern=[[0, HEADS], [1, P]], compare_op=ALU.is_ge,
                            fill=0.0, base=0, channel_multiplier=-1).then_inc(wm_ready, 1)

            e.wait_ge(wm_ready, 2)

            def mask(t, ready, n):
                v = t[:, :, :].rearrange("p h (a b) -> p h a b", a=2)[:, :, :, 0:P]
                e.affine_select(out=v, in_=v, pattern=[[0, 2], [0, 2], [1, P]], compare_op=ALU.is_gt,
                                fill=0.0, base=0, channel_multiplier=-1).then_inc(ready, 1)
                e.wait_ge(ready, n)

            for p in range(4):
                e.wait_ge(sp_ready, p + 1)
                mask(sp, sp_masked, p + 1)
                e.wait_ge(att_exp, p + 1)
                mask(att, att_ready, p + 1)

        @block.scalar
        def _(act):
            e = act
            ch = Chain(e, act_self)

            def high(g, static_g, words, landed):
                slot, unit_slot = static_g % SPLIT_SLOTS, raw_unit(static_g) % RAW_SLOTS
                e.wait_ge(raw_in[unit_slot], landed)
                e.wait_ge(w_used, g + 1)
                e.activation(w_hi[:, slot, 0:words], raw[:, unit_slot, 0:words], ACT.Copy).then_inc(w_high, 1)

            def high_at(g):
                if g < len(STAGE_OF):
                    high(g, g, WORDS[STAGE_OF[g]], landed_at(raw_unit(g)))

            def run(stage, step, per=0):
                n, g0 = N_BLOCKS[stage], FIRST[stage]
                last = max((n - 4) // 4, 1)
                k = 2 if stage == "sc_in" else 1
                for b in range(4):
                    high_at(g0 + b + AHEAD)
                    step(0, b)
                if last > 1:
                    with ch.loop(1, last, per) as it:
                        for b in range(4):
                            g = g0 + b + AHEAD
                            high(it * 4 + g, g, WORDS[stage], it * (16 * k) + landed_at(raw_unit(g)))
                            step(it, b)
                for j in range(4 * last, n):
                    high_at(g0 + j + AHEAD)
                    step(j // 4, j % 4)

            def square(number, src):
                if number >= 2:
                    e.wait_ge(sq_used, number - 1)
                e.activation(sq[:, number % 2, :], src, ACT.Square).then_inc(sq_ready, 1)

            def inverse_rms(number, pairs_summed, width, count):
                e.wait_ge(sq_used, pairs_summed)
                if number - 2 in range(STATN["qk"], STATN["qk"] + 4):
                    e.wait_ge(qk_ready, number - 1 - STATN["qk"])
                r = rstd[:, number % 2, 0:width]
                if count == D:
                    e.activation(r, ps[:, STAT, 0:width], ACT.Sqrt, bias=eps[:, :], scale=1.0 / count).then_inc(rstd_ready, 1)
                    return
                ch.link(e.activation(r, ps[:, STAT, 0:width], ACT.Ln, bias=eps[:, :], scale=1.0 / count))
                e.activation(r, r, ACT.Exp, scale=-0.5).then_inc(rstd_ready, 1)

            def act_high(norm, shift):
                for i in range(DT):
                    e.wait_ge(norm_t, ACT_TILE[norm] + i + 1)
                    if shift is None:
                        ins = e.activation(a_hi[:, i, :], y[:, i, :], ACT.Copy)
                    else:
                        ins = e.activation(a_hi[:, i, :], y[:, i, :], ACT.Identity,
                                           bias=mod[:, shift * DT + i:shift * DT + i + 1])
                    ins.then_inc(act_hi, 1)

            def x_norm(norm, shift):
                for t in range(4):
                    e.wait_ge(x_new, X_NEW[norm] + 2 * t + 2)
                    square(SQ[norm] + t, flat(x[:, 2 * t:2 * t + 2, :]))
                inverse_rms(STATN[norm], SQ[norm] + 4, T, D)
                act_high(norm, shift)

            e.wait_ge(par_in, 16)
            e.wait_ge(const_set, 1)
            e.activation(silu_c[:, :], pcol("c", 0, 8), ACT.Silu).then_inc(c_ready, 1)
            e.wait_ge(x_landed, 16)
            for t in range(4):
                square(SQ["x"] + t, flat(x[:, 2 * t:2 * t + 2, :]))
            inverse_rms(STATN["x"], SQ["x"] + 4, T, D)
            high_at(0)
            high_at(1)
            e.wait_ge(mod_read, 2)
            act_high("x", 0)
            for g in range(2, AHEAD):
                high_at(g)

            def sc_first(grp, pb):
                e.wait_ge(w_used, grp * 2 + (2 + FIRST["sc_in"] + USED))
                e.activation(sc_c[:, pb, :], ps[:, 2 * pb, 0:T], ACT.Copy).then_inc(sc_c_ready, 1)
                e.wait_ge(sc_cv_ready, grp + 1)
                e.activation(sc_u[:, pb, :], sc_cv[:, pb, 1:T + 1], ACT.Copy,
                             scale=pdyn("sc_conv", grp * 3 + 1)).then_inc(sc_u_ready, 1)

            def sc_high(grp, pb):
                e.wait_ge(free["sc_in"], grp + (1 + CREDIT["sc_in"]))
                e.activation(row(sc_hi, grp), sc_y[:, pb, :], ACT.Copy).then_inc(sc_hi_ready, 1)

            def sc_in_step(it, b):
                if isinstance(it, int) and 4 * it + b < 2:
                    return
                grp, pb = it * 2 + (b // 2 - 1), 1 - b // 2
                (sc_high if b % 2 else sc_first)(grp, pb)
                if isinstance(it, int) and 4 * it + b == N_BLOCKS["sc_in"] - 1:
                    sc_first(grp + 1, 1 - pb)
                    sc_high(grp + 1, 1 - pb)

            run("sc_in", sc_in_step)

            def sc_out_step(it, b):
                j = 4 * it + b
                e.wait_ge(w_used, FIRST["sc_out"] + j + 1 + USED)
                square(SQ["post"] + j, ps[:, b, :])

            run("sc_out", sc_out_step)
            inverse_rms(STATN["post"], SQ["post"] + 4, T, D)
            x_norm("pre_ff", 3)

            def mlp_in_step(it, b):
                e.wait_ge(w_used, it * 4 + (FIRST["mlp_in"] + b + 1 + USED))
                if not (isinstance(it, int) and 4 * it + b < 2):
                    e.wait_ge(hid_split, it * 4 + (b - 1))
                e.activation(hid[:, b % 2, :], ps[:, b, :], ACT.Relu).then_inc(free["mlp_in"], 1)
                e.wait_ge(free["mlp_in"], it * 4 + (b + 1 + CREDIT["mlp_in"]))
                e.activation(hid[:, b % 2, :], hid[:, b % 2, :], ACT.Square).then_inc(hid_ready, 1)

            run("mlp_in", mlp_in_step)

            def mlp_out_step(it, b):
                if b == 3:
                    e.wait_ge(w_used, it * 4 + (FIRST["mlp_out"] + b + 1 + USED))
                    square(SQ["post_ff"] + it, ps[:, it % 2, :])

            for j in range(N_BLOCKS["mlp_out"]):
                high_at(FIRST["mlp_out"] + j + AHEAD)
                mlp_out_step(j // 4, j % 4)
            inverse_rms(STATN["post_ff"], SQ["post_ff"] + 4, T, D)
            x_norm("ln1", None)

            def softplus_log(p):
                zb = Z_BANKS[p % 2]
                e.wait_ge(z_done, p + 1)
                if p:
                    e.wait_ge(sp_ready, p)
                ch.link(e.activation(sp_t[:, :, :], ps[:, zb:zb + 2, 0:384], ACT.Abs))
                ch.link(e.activation(sp_t[:, :, :], sp_t[:, :, :], ACT.Exp, scale=-1.0))
                e.activation(sp_t[:, :, :], sp_t[:, :, :], ACT.Ln, bias=1.0).then_inc(sp_log, 1)

            def weights(p):
                e.wait_ge(loga_low, p + 1)
                e.activation(att[:, :, 0:384], att[:, :, 0:384], ACT.Exp).then_inc(att_exp, 1)

            for s, kind in enumerate(Z_ORDER):
                g = FIRST["z_in"] + s
                high_at(g + AHEAD)
                bank = Z_FILL[s] % 2 if s in Z_FILL else None
                if kind in ("q", "k", "pg", "u", "gate"):
                    e.wait_ge(w_used, g + 1 + USED)
                if kind in ("q", "k"):
                    t = s - QK_FIRST
                    square(SQ["qk"] + t, ps[:, bank, :])
                    e.activation(flat(y[:, 2 * t:2 * t + 2, :]), ps[:, bank, :], ACT.Copy).then_inc(qk_raw, 1)
                if 1 <= s - QK_FIRST <= 4:
                    t = s - QK_FIRST - 1
                    inverse_rms(STATN["qk"] + t, SQ["qk"] + t + 1, 2 * T, 64)
                if kind == "vv" and Z_ORDER[s + 1] != "vv":
                    e.wait_ge(w_used, g + 1 + USED)
                    for c in range(2):
                        e.activation(vv[:, c, :], ps[:, TOKEN_BANK + c, :], ACT.Copy).then_inc(vv_ready, 1)
                if kind == "pg":
                    i = s - Z_ORDER.index("pg")
                    if i >= 2:
                        e.wait_ge(c_in, i - 1)
                    e.activation(sig[:, i % 2, :], ps[:, bank, T:2 * T], ACT.Sigmoid).then_inc(sig_ready, 1)
                if kind == "v" and Z_ORDER[s + 1] != "v":
                    e.wait_ge(w_used, g + 1 + USED)
                    for c in range(2):
                        e.activation(vg[:, c, :], ps[:, TOKEN_BANK + c, :], ACT.Gelu_apprx_tanh).then_inc(vg_ready, 1)
                if kind == "u":
                    i = s - Z_ORDER.index("u")
                    e.activation(flat(u_sb[:, 2 * i:2 * i + 2, :]), ps[:, bank, :],
                                 ACT.Gelu_apprx_tanh).then_inc(z_free_act, 1)
                if s == VLN_STEP:
                    e.wait_ge(vg_var, 2)
                    for c in range(2):
                        ch.mark(e.activation(vstd[:, c:c + 1], bn[:, c, 7:8], ACT.Ln, bias=eps[:, :]))
                    ch.wait()
                    for c in range(2):
                        e.activation(vstd[:, 2 + c:3 + c], vstd[:, c:c + 1], ACT.Exp, scale=-0.5).then_inc(vg_std, 1)
                if kind == "gate":
                    for h in range(2):
                        n = 2 * (s - Z_ORDER.index("gate")) + h
                        ins = e.activation(gates[:, n, :], ps[:, bank, h * T:(h + 1) * T], ACT.Identity,
                                           bias=pcol("b_gate", n))
                        ch.mark(ins) if h == 0 else ins.then_inc(z_free_act, 1)
                for p in range(4):
                    if s == U_STEP(p):
                        weights(p)
                for p in range(4):
                    if s == QK_STEP(p):
                        softplus_log(p)
                if s == CV_VAR_STEP:
                    for t in range(2):
                        e.wait_ge(cv_cent, 2 * t + 2)
                        square(SQ["cv"] + t, flat(cacc[:, 2 * t:2 * t + 2, :]))
                    inverse_rms(STATN["cv"], SQ["cv"] + 2, T, SG)
                    for i in range(4):
                        e.wait_ge(cv_norm, i + 1)
                        e.activation(cacc[:, i, :], cacc[:, i, :], ACT.Silu, bias=pcol("cv_lb", i)).then_inc(cv_silu, 1)
            e.wait_ge(z_free_act, 14)
            ch.wait()
            e.activation(flat(gates[:, 0:6, :]), flat(gates[:, 0:6, :]), ACT.Sigmoid).then_inc(gates_ready, 1)
            e.activation(flat(gates[:, 6:24, :]), flat(gates[:, 6:24, :]), ACT.Sigmoid).then_inc(gates_ready, 1)

            def mix_high(j):
                e.wait_ge(mix_sum, j + 1)
                e.activation(a_hi[:, j, :], mg_t[:, 0, :], ACT.Copy).then_inc(mix_hi, 1)

            for j in range(N_BLOCKS["branch"]):
                high_at(FIRST["branch"] + j + AHEAD)
                if j:
                    mix_high(j - 1)
            mix_high(N_BLOCKS["branch"] - 1)
            for j in range(N_BLOCKS["mix_out"]):
                high_at(FIRST["mix_out"] + j + AHEAD)
            x_norm("ln2", None)

            def silu_gate(it, b):
                e.wait_ge(free["up"], it * 4 + (b + 1 + CREDIT["up"]))
                if not (isinstance(it, int) and 4 * it + b < 2):
                    e.wait_ge(up_ready, it * 4 + (b - 1))
                e.activation(up_g[:, b % 2, :], up_u[:, b % 2, 0:T], ACT.Silu).then_inc(up_g_ready, 1)

            def up_step(it, b):
                e.wait_ge(w_used, it * 4 + (FIRST["up"] + b + 1 + USED))
                if not (isinstance(it, int) and 4 * it + b < 2):
                    e.wait_ge(up_ready, it * 4 + (b - 1))
                for h in range(2):
                    e.activation(up_u[:, b % 2, h * T:(h + 1) * T], ps[:, b, h * T:(h + 1) * T], ACT.Identity,
                                 bias=pdyn("up_b", it * 8 + (2 * b + h)),
                                 scale=pdyn("up_w", it * 24 + (3 * (2 * b + h) + 2))).then_inc(up_u_ready, 1)
                if isinstance(it, int):
                    if 4 * it + b >= 1:
                        silu_gate((4 * it + b - 1) // 4, (b - 1) % 4)
                else:
                    silu_gate(it - 1, 3) if b == 0 else silu_gate(it, b - 1)

            run("up", up_step)
            silu_gate(5, 1)
            for j in range(N_BLOCKS["down"]):
                high_at(FIRST["down"] + j + AHEAD)

        @block.vector
        def _(dve):
            e = dve
            ch = Chain(e, dve_self)

            def low(g, static_g, words):
                slot, unit_slot = static_g % SPLIT_SLOTS, raw_unit(static_g) % RAW_SLOTS
                e.wait_ge(w_high, g + 1)
                e.tensor_tensor(w_lo[:, slot, 0:words], raw[:, unit_slot, 0:words],
                                w_hi[:, slot, 0:words].bitcast(f32), SUB).then_inc(raw_used, 1)

            def ada_part(src, col, acc):
                return e.scalar_tensor_tensor(acc, src, col, acc, MUL, ADD)

            def ada_unit(u, k, acc):
                e.wait_ge(raw_in[u % RAW_SLOTS], landed_at(u))
                if u:
                    e.wait_ge(raw_used, u)
                src = raw[:, u % RAW_SLOTS, :]
                if k == 0:
                    ch.link(e.tensor_scalar(acc, src[:, 0:D], silu_c[:, 0:1], None, MUL))
                else:
                    ch.link(ada_part(src[:, 0:D], silu_c[:, k:k + 1], acc))
                ada_part(src[:, D:2 * D], silu_c[:, k + 1:k + 2], acc).then_inc(raw_used, 1)

            def ada_half_unit(unit, static_unit, landed, acc, col):
                e.wait_ge(raw_in[static_unit % RAW_SLOTS], landed)
                e.wait_ge(raw_used, unit)
                ada_part(raw[:, static_unit % RAW_SLOTS, 0:D], col, acc).then_inc(raw_used, 1)

            def ahead_at(g, between=lambda: None):
                if g < len(STAGE_OF):
                    low(g, g, WORDS[STAGE_OF[g]])
                between()
                ada_after(g)

            def ada_after(g):
                u = raw_unit(g) + 1
                if g in ADA_AFTER["sc_in"]:
                    ada_half_unit(u, u, landed_at(u), ada_acc[:, 2 + g % 2, :], silu_c[:, g // 2:g // 2 + 1])
                if g in ADA_AFTER["sc_out"]:
                    ada_unit(u, 2 * (g - 17), ada_acc[:, 4, :])
                if g in ADA_AFTER["mlp_out"]:
                    ada_unit(u, 2 * (g - 40), hid[:, :, :].rearrange("p a b -> p (a b)"))

            def run(stage, step, per=0, between=lambda it, b: None):
                n, g0 = N_BLOCKS[stage], FIRST[stage]
                last = max((n - 4) // 4, 1)
                for b in range(4):
                    ahead_at(g0 + b + AHEAD, lambda: between(0, b))
                    step(0, b)
                if last > 1:
                    with ch.loop(1, last, per) as it:
                        for b in range(4):
                            g = g0 + b + AHEAD
                            low(it * 4 + g, g, WORDS[stage])
                            between(it, b)
                            if stage == "sc_in":
                                u = raw_unit(g) + 1
                                ada_half_unit(it * 8 + u, u, it * 32 + landed_at(u), ada_acc[:, 2 + g % 2, :],
                                              silu_c[:, bass.ds(it * 2 + g // 2, 1)])
                            step(it, b)
                for j in range(4 * last, n):
                    ahead_at(g0 + j + AHEAD, lambda: between(j // 4, j % 4))
                    step(j // 4, j % 4)

            def inverse_rms(number, width=T):
                e.wait_ge(rstd_ready, number + 1)
                r = rstd[:, number % 2, 0:width]
                if number not in range(STATN["qk"], STATN["cv"] + 1):
                    ch.link(e.reciprocal(r, r))
                return r

            def split(hi, lo, src, ready):
                ch.link(e.tensor_copy(hi, src))
                e.tensor_tensor(lo, src, hi.bitcast(f32), SUB).then_inc(ready, 1)

            def low_part(norm, i, shift):
                e.wait_ge(act_hi, ACT_TILE[norm] + i + 1)
                e.scalar_tensor_tensor(a_lo[:, i, :], y[:, i, :],
                                       0.0 if shift is None else mod[:, shift * DT + i:shift * DT + i + 1],
                                       a_hi[:, i, :].bitcast(f32), ADD, SUB).then_inc(act_lo, 1)

            def normalise(norm, gain, shift):
                scale = inverse_rms(STATN[norm])
                for i in range(DT):
                    e.scalar_tensor_tensor(y[:, i, :], x[:, i, :], gain(i), scale, MUL, MUL).then_inc(norm_t, 1)
                    if i >= 2:
                        low_part(norm, i - 2, shift)
                low_part(norm, DT - 2, shift)
                low_part(norm, DT - 1, shift)

            def post_norm(norm, gain):
                scale = inverse_rms(STATN[norm])
                start = ch.n
                for i in range(DT + 1):
                    if i < DT:
                        ch.mark(e.scalar_tensor_tensor(y[:, i, :], y[:, i, :], gain[:, i:i + 1], scale, MUL, MUL))
                    if i >= 1:
                        ch.wait(start + i)
                        ins = e.tensor_tensor(x[:, i - 1, :], x[:, i - 1, :], y[:, i - 1, :], ADD)
                        ins.then_inc(x_new, 1)

            MOD_SUMMED = (1, 2, 4, 4, 5, 6)

            def mods(number, vector):
                e.wait_ge(mod_ps, MOD_SUMMED[number])
                cols = slice(8 * vector, 8 * vector + 8)
                e.tensor_tensor(mod[:, cols], ps[:, MISC, cols], pcol("ada_b", 8 * vector, 8), ADD).then_inc(mod_read, 1)
                e.wait_ge(mod_read, number + 1)

            e.wait_ge(c_ready, 1)
            for i in range(4):
                ada_unit(i, 2 * i, ada_acc[:, 1, :])
            x_scale = inverse_rms(STATN["x"])
            for i in range(2):
                ada_unit(4 + i, 2 * i, ada_acc[:, 0, :])
            mods(0, 1)
            ch.link(e.scalar_tensor_tensor(gain_pre[:, :], mod[:, 8:16], 1.0, pcol("gains", 0, 8), ADD, MUL))
            for i in range(2, 4):
                ada_unit(4 + i, 2 * i, ada_acc[:, 0, :])
            for i in range(DT):
                e.scalar_tensor_tensor(y[:, i, :], x[:, i, :], gain_pre[:, i:i + 1], x_scale, MUL, MUL)\
                 .then_inc(norm_t, 1)
            low(0, 0, WORDS["sc_in"])
            mods(1, 0)
            for i in range(DT):
                low_part("x", i, 0)
            e.wait_ge(const_set, 4)
            ada_after(0)
            for g in range(1, AHEAD):
                ahead_at(g)

            def sc_first(grp, pb):
                e.wait_ge(sc_c_ready, grp + 1)
                e.tensor_tensor(sc_cv[:, pb, 1:T + 1], ps[:, 2 * pb, T:2 * T], sc_c[:, pb, :], MUL).then_inc(sc_cv_ready, 1)

            def sc_rest(grp, pb):
                u, cv = sc_u[:, pb, :], sc_cv[:, pb, :]
                e.wait_ge(sc_u_ready, grp + 1)
                ch.link(e.scalar_tensor_tensor(u, cv[:, 0:T], pdyn("sc_conv", grp * 3), u, MUL, ADD))
                ch.link(e.scalar_tensor_tensor(u, cv[:, 2:T + 2], pdyn("sc_conv", grp * 3 + 2), u, MUL, ADD))
                e.tensor_tensor(sc_y[:, pb, :], u, ps[:, 2 * pb + 1, 0:T], MUL).then_inc(free["sc_in"], 1)

            def sc_low(grp, pb):
                e.wait_ge(sc_hi_ready, grp + 1)
                e.tensor_tensor(row(sc_lo, grp), sc_y[:, pb, :], row(sc_hi, grp).bitcast(f32), SUB).then_inc(sc_ready, 1)

            def group_at(it, b):
                return it * 2 + (b // 2 - 1), 1 - b // 2

            def sc_between(it, b):
                if isinstance(it, int) and 4 * it + b == N_BLOCKS["sc_in"] - 1:
                    grp, pb = group_at(it, b)
                    sc_low(grp, pb)
                    sc_first(grp + 1, 1 - pb)
                    sc_rest(grp + 1, 1 - pb)
                    sc_low(grp + 1, 1 - pb)
                elif b % 2 == 0 and not (isinstance(it, int) and 4 * it + b < 2):
                    sc_first(*group_at(it, b))

            def sc_in_step(it, b):
                if isinstance(it, int) and (4 * it + b < 2 or 4 * it + b == N_BLOCKS["sc_in"] - 1):
                    return
                (sc_low if b % 2 else sc_rest)(*group_at(it, b))

            run("sc_in", sc_in_step, 4, sc_between)

            def raw_copy(stage, sq_number, pair, bank, inc=None):
                e.wait_ge(sq_ready, sq_number + 1)
                ins = e.tensor_copy(flat(y[:, 2 * pair:2 * pair + 2, :]), ps[:, bank, :])
                ins.then_inc(inc, 1) if inc is not None else ch.mark(ins)

            run("sc_out", lambda it, b: raw_copy("sc_out", SQ["post"] + b, b, b))
            mods(2, 2)
            mods(3, 4)
            ch.mark(e.tensor_tensor(gain_post[:, :], mod[:, 16:24], pcol("gains", 8, 8), MUL))
            ch.link(e.scalar_tensor_tensor(gain_pre_ff[:, :], mod[:, 32:40], 1.0, pcol("gains", 16, 8), ADD, MUL))
            post_norm("post", gain_post)
            mods(4, 3)
            normalise("pre_ff", lambda i: gain_pre_ff[:, i:i + 1], 3)

            def mlp_in_step(it, b):
                e.wait_ge(hid_ready, it * 4 + (b + 1))
                pair = bass.ds(it * 8 + 2 * b, 2)
                split(hid_hi[:, pair, :], hid_lo[:, pair, :], hid[:, b % 2, :].rearrange("p (a c) -> p a c", a=2), hid_split)

            run("mlp_in", mlp_in_step, 4)
            for j in range(N_BLOCKS["mlp_out"]):
                ahead_at(FIRST["mlp_out"] + j + AHEAD)
                if j % 4 == 3:
                    t = j // 4
                    raw_copy("mlp_out", SQ["post_ff"] + t, t, t % 2, free["mlp_out"])
            mods(5, 5)
            ch.link(e.tensor_tensor(gain_post_ff[:, :], mod[:, 40:48], pcol("gains", 24, 8), MUL))
            e.wait_ge(free["mlp_out"], 4 + CREDIT["mlp_out"])
            post_norm("post_ff", gain_post_ff)
            normalise("ln1", lambda i: pcol("ln1", i), None)

            ch.link(e.tensor_scalar(qk_gain[:, 0:1], pcol("qk_g", 0), 0.125, None, MUL))

            def conv(lo_step, hi_step):
                for n in range(lo_step, hi_step):
                    i, tap = 2 * (n // (2 * CV_TAPS)) + n % 2, n % (2 * CV_TAPS) // 2
                    src, wt = cpad[:, i, tap:tap + T], pcol("cv_w", CV_TAPS * i + tap)
                    if tap == 0:
                        e.wait_ge(c_in, i + 1)
                        e.wait_ge(wm_ready, 2)
                        e.tensor_scalar(cacc[:, i, :], src, wt, pcol("cv_b", i), MUL, ADD).then_inc(conv_step, 1)
                    else:
                        e.wait_ge(conv_step, n - 1)
                        e.scalar_tensor_tensor(cacc[:, i, :], src, wt, cacc[:, i, :], MUL, ADD).then_inc(conv_step, 1)

            def softplus(p):
                e.wait_ge(sp_log, p + 1)
                if p:
                    e.wait_ge(loga_done, p)
                zb = Z_BANKS[p % 2]
                e.scalar_tensor_tensor(sp[:, :, 0:384], ps[:, zb:zb + 2, 0:384], 0.0, sp_t[:, :, :], MAX, ADD)\
                 .then_inc(sp_ready, 1)

            def clamp(p):
                e.wait_ge(loga_done, p + 1)
                if p:
                    e.wait_ge(att_done, p)
                zb = Z_BANKS[p % 2]
                e.tensor_scalar(att[:, :, 0:384], ps[:, zb:zb + 2, 0:384], 0.0, None, ALU.min).then_inc(loga_low, 1)

            def att_out(p):
                e.wait_ge(att_done, p + 1)
                split(br["c"][0][:, p, :], br["c"][1][:, p, :], ps[:, MISC, T * (p % 2):T * (p % 2) + T], br_c)

            for s, kind in enumerate(Z_ORDER):
                g = FIRST["z_in"] + s
                ahead_at(g + AHEAD)
                bank = Z_FILL[s] % 2 if s in Z_FILL else None
                if 1 <= s - QK_FIRST <= 4:
                    t = s - QK_FIRST - 1
                    scale = inverse_rms(STATN["qk"] + t, 2 * T)
                    e.wait_ge(qk_raw, t + 1)
                    gain = qk_gain[:, 0:1] if t < 2 else pcol("qk_g", 1)
                    pair = flat(y[:, 2 * t:2 * t + 2, :])
                    e.scalar_tensor_tensor(pair, pair, gain, scale, MUL, MUL).then_inc(qk_ready, 1)
                if kind == "pg":
                    i = s - Z_ORDER.index("pg")
                    e.wait_ge(sig_ready, i + 1)
                    e.tensor_tensor(cpad[:, i, CV_TAPS - 1:], ps[:, bank, 0:T], sig[:, i % 2, :], MUL).then_inc(c_in, 1)
                if kind == "v" and Z_ORDER[s + 1] != "v":
                    for c in range(2):
                        e.wait_ge(vg_ready, c + 1)
                        ch.link(e.bn_stats(bn[:, c, 0:6], vg[:, c, :]))
                        e.bn_aggr(bn[:, c, 6:8], bn[:, c, 0:6]).then_inc(vg_var, 1)
                if s == VLN_STEP:
                    e.wait_ge(vg_std, 2)
                    e.wait_ge(wm_ready, 2)
                    for c in range(2):
                        v = vg[:, c, :]
                        ch.link(e.tensor_scalar(v, v, bn[:, c, 6:7], vstd[:, 2 + c:3 + c], SUB, MUL))
                        ch.link(e.tensor_tensor(v, v, sgln[:, 0, :], MUL))
                        e.tensor_tensor(v, v, sgln[:, 1, :], ADD).then_inc(vln_ready, 1)
                if s == SG_STEP:
                    e.wait_ge(sg_done, 1)
                    e.wait_ge(z_free_act, 2)
                    for t in range(4):
                        o = sgo[:, t, :]
                        for c in range(2):
                            ch.mark(e.tensor_tensor(o[:, c * P:(c + 1) * P],
                                                    ps[:, SG_BANK + t // 2, T * (t % 2) + c * P:T * (t % 2) + (c + 1) * P],
                                                    sgb[:, t, :], ADD))
                        ch.wait()
                        ch.link(e.tensor_tensor(o, o, u_sb[:, t, :], MUL))
                        split(br["a"][0][:, t, :], br["a"][1][:, t, :], o, br_a)
                if s in CONV_AT:
                    first = sum(n for step, n in CONV_AT.items() if step < s)
                    conv(first, first + CONV_AT[s])
                for p in range(4):
                    if s == U_STEP(p):
                        clamp(p)
                for p in range(4):
                    if s == QK_STEP(p):
                        softplus(p)
                    if s == AV_STEP(p):
                        att_out(p)
                if s == CV_MEAN_STEP:
                    e.wait_ge(cv_mean, 1)
                    for i in range(4):
                        e.scalar_tensor_tensor(cacc[:, i, :], ps[:, STAT, 0:T], -1.0 / SG, cacc[:, i, :], MUL, ADD)\
                         .then_inc(cv_cent, 1)
                if s == CV_VAR_STEP:
                    scale = inverse_rms(STATN["cv"])
                    for i in range(4):
                        e.scalar_tensor_tensor(cacc[:, i, :], cacc[:, i, :], pcol("cv_g", i), scale, MUL, MUL)\
                         .then_inc(cv_norm, 1)
                    for i in range(4):
                        e.wait_ge(cv_silu, i + 1)
                        split(br["b"][0][:, i, :], br["b"][1][:, i, :], cacc[:, i, :], br_b)

            def mix_low(j):
                e.wait_ge(mix_hi, j + 1)
                e.tensor_tensor(a_lo[:, j, :], mg_t[:, 0, :], a_hi[:, j, :].bitcast(f32), SUB).then_inc(mix_ready, 1)

            for j in range(N_BLOCKS["branch"]):
                ahead_at(FIRST["branch"] + j + AHEAD)
                if j:
                    mix_low(j - 1)
                e.wait_ge(w_used, FIRST["branch"] + j + 1 + USED)
                e.wait_ge(gates_ready, 1 if j < 2 else 2)
                if j:
                    e.wait_ge(mix_ready, j)
                bk = 2 * (j % 2)
                ch.mark(e.tensor_tensor(flat(mg_t[:, 0:2, :]), ps[:, bk, :], flat(gates[:, 3 * j:3 * j + 2, :]), MUL))
                e.tensor_tensor(mg_t[:, 2, :], ps[:, bk + 1, 0:T], gates[:, 3 * j + 2, :], MUL).then_inc(free["branch"], 1)
                ch.wait()
                m = mg_t[:, 0, :]
                ch.link(e.tensor_tensor(m, m, mg_t[:, 1, :], ADD))
                e.wait_ge(free["branch"], j + 1 + CREDIT["branch"])
                e.tensor_tensor(m, m, mg_t[:, 2, :], ADD).then_inc(mix_sum, 1)
            mix_low(N_BLOCKS["branch"] - 1)
            for j in range(N_BLOCKS["mix_out"]):
                ahead_at(FIRST["mix_out"] + j + AHEAD)
                e.wait_ge(w_used, FIRST["mix_out"] + j + 1 + USED)
                pair = flat(x[:, 2 * j:2 * j + 2, :])
                e.tensor_tensor(pair, pair, ps[:, j, :], ADD).then_inc(x_new, 2)
            e.wait_ge(x_new, X_NEW["ln2"] + DT)
            normalise("ln2", lambda i: pcol("ln2", i), None)

            def product(it, b):
                e.wait_ge(up_g_ready, it * 4 + (b + 1))
                ch.link(e.tensor_tensor(up_p[:, b % 2, :], up_g[:, b % 2, :], up_u[:, b % 2, T:2 * T], MUL))
                i = it * 4 + b
                split(row(up_hi, i), row(up_lo, i), up_p[:, b % 2, :], up_ready)

            def up_step(it, b):
                e.wait_ge(up_u_ready, it * 8 + (2 * b + 2))
                for tap in (1, 0):
                    for h in range(2):
                        o = 2 - tap
                        dst = up_u[:, b % 2, h * T + o:(h + 1) * T]
                        ins = e.scalar_tensor_tensor(dst, ps[:, b, h * T:(h + 1) * T - o],
                                                     pdyn("up_w", it * 24 + (3 * (2 * b + h) + tap)), dst, MUL, ADD)
                        if tap == 0 and h == 1:
                            ins.then_inc(free["up"], 1)
                        else:
                            ch.mark(ins)
                    if tap == 1:
                        ch.wait()
                if isinstance(it, int):
                    if 4 * it + b >= 1:
                        product((4 * it + b - 1) // 4, (b - 1) % 4)
                else:
                    product(it - 1, 3) if b == 0 else product(it, b - 1)

            run("up", up_step, 4 * 5)
            product(5, 1)
            for j in range(N_BLOCKS["down"]):
                ahead_at(FIRST["down"] + j + AHEAD)
                if j % 4 == 3:
                    t = j // 4
                    e.wait_ge(w_used, FIRST["down"] + j + 1 + USED)
                    pair = flat(x[:, 2 * t:2 * t + 2, :])
                    e.tensor_tensor(pair, pair, ps[:, 2 + t % 2, :], ADD).then_inc(out_ready, 1)

        @block.tensor
        def _(pe):
            e = pe

            def product(dst, slot, tile, hi, lo, start, stop, skip=False):
                cols = slice(tile * P, (tile + 1) * P)
                e.matmul(dst, w_hi[:, slot, cols], hi, start=start, stop=False, skip_group_check=skip)
                e.matmul(dst, w_hi[:, slot, cols], lo, start=False, stop=False, skip_group_check=skip)
                return e.matmul(dst, w_lo[:, slot, cols], hi, start=False, stop=stop, skip_group_check=skip)

            def half(bank, h):
                return ps[:, bank, h * T:(h + 1) * T]

            def sum_squares(number, stat, first, last):
                e.wait_ge(sq_ready, number + 1)
                if first and stat:
                    e.wait_ge(rstd_ready, stat)
                for h in range(2):
                    mm = e.matmul(ps[:, STAT, 0:T], ones[:, :], sq[:, number % 2, h * T:(h + 1) * T],
                                  start=first and h == 0, stop=last and h == 1)
                mm.then_inc(sq_used, 1)

            def mod_sum(vector, acc, i):
                n = DT * vector + i
                mm = e.matmul(ps[:, MISC, n:n + 1], acc[:, i * P:(i + 1) * P], ones[:, 0:1], start=True, stop=True)
                if i == DT - 1:
                    mm.then_inc(mod_ps, 1)

            def mod_sums(vector, acc):
                for i in range(DT):
                    mod_sum(vector, acc, i)

            e.wait_ge(const_set, 2)
            for t in range(4):
                sum_squares(SQ["x"] + t, STATN["x"], t == 0, t == 3)
            e.wait_ge(raw_used, 4)
            mod_sums(1, ada_acc[:, 1, :])
            e.wait_ge(raw_used, ADA_FIRST)
            e.wait_ge(mod_read, 1)
            mod_sums(0, ada_acc[:, 0, :])

            g0 = FIRST["sc_in"]

            def sc_in_block(it, b):
                if b % 2 == 0:
                    e.wait_ge(free["sc_in"], it * 2 + (b // 2 + 1))
                e.wait_ge(raw_used, it * 8 + (raw_unit(g0 + b) + 1))
                for t in range(12):
                    n, k = divmod(12 * (b % 2) + t, DT)
                    dst = half(2 * (b // 2) + n // 2, n % 2)
                    mm = product(dst, (g0 + b) % SPLIT_SLOTS, t, a_hi[:, k, :], a_lo[:, k, :], k == 0, k == DT - 1,
                                 isinstance(it, int) and b == 1)
                mm.then_inc(w_used, 1)

            e.wait_ge(free["sc_in"], 1)
            e.wait_ge(raw_used, raw_unit(g0) + 1)
            for k in range(DT):
                e.wait_ge(act_lo, ACT_TILE["x"] + k + 1)
                for n in range(2 if k < 4 else 1):
                    mm = product(half(0, n), g0 % SPLIT_SLOTS, n * DT + k, a_hi[:, k, :], a_lo[:, k, :],
                                 k == 0 and n == 0, k == DT - 1, True)
            mm.then_inc(w_used, 1)
            for b in range(1, 4):
                sc_in_block(0, b)
            with e.Fori(1, N_BLOCKS["sc_in"] // 4) as it:
                for b in range(4):
                    sc_in_block(it, b)

            def pair_block(g, static_g, banks, hi, lo, between=lambda t: None):
                e.wait_ge(raw_used, g)
                for t in range(16):
                    n, k = divmod(t, DT)
                    mm = product(half(banks, n), static_g % SPLIT_SLOTS, t, hi[:, k, :], lo[:, k, :], k == 0, k == DT - 1)
                    if t < 15:
                        between(t)
                mm.then_inc(w_used, 1)
                between(15)

            def first_block(ready, before, g, static_g, bank, hi, lo):
                e.wait_ge(raw_used, g)
                for k in range(DT):
                    e.wait_ge(ready, before + k + 1)
                    for n in range(2):
                        mm = product(half(bank, n), static_g % SPLIT_SLOTS, n * DT + k, hi[:, k, :], lo[:, k, :],
                                     k == 0 and n == 0, k == DT - 1, True)
                mm.then_inc(w_used, 1)

            g0 = FIRST["sc_out"]
            for j in range(4):
                if j == 2:
                    e.wait_ge(raw_used, raw_unit(g0))
                    e.wait_ge(mod_read, 2)
                    pair_block(raw_unit(g0 + j) + 1, g0 + j, j, sc_hi, sc_lo,
                               lambda t: mod_sum(2 + 2 * (t // DT), ada_acc[:, 2 + t // DT, :], t % DT))
                elif j == 0:
                    e.wait_ge(free["sc_in"], DT - 1 + CREDIT["sc_in"])
                    first_block(sc_ready, 0, raw_unit(g0) + 1, g0, 0, sc_hi, sc_lo)
                else:
                    pair_block(raw_unit(g0 + j) + 1, g0 + j, j, sc_hi, sc_lo)
                if j >= 1:
                    sum_squares(SQ["post"] + j - 1, STATN["post"], j == 1, False)
            sum_squares(SQ["post"] + 3, STATN["post"], False, True)
            e.wait_ge(raw_used, raw_unit(g0 + 5))
            e.wait_ge(mod_read, 4)
            mod_sums(3, ada_acc[:, 4, :])

            def x_norm(norm):
                for t in range(4):
                    sum_squares(SQ[norm] + t, STATN[norm], t == 0, t == 3)

            x_norm("pre_ff")
            g0 = FIRST["mlp_in"]
            for b in range(4):
                e.wait_ge(free["mlp_in"], b + 1)
                if b == 0:
                    first_block(act_lo, ACT_TILE["pre_ff"], raw_unit(g0) + 1, g0, 0, a_hi, a_lo)
                else:
                    pair_block(raw_unit(g0 + b) + 1, g0 + b, b, a_hi, a_lo)
            with e.Fori(1, N_BLOCKS["mlp_in"] // 4) as it:
                for b in range(4):
                    e.wait_ge(free["mlp_in"], it * 4 + (b + 1))
                    pair_block(it * 4 + (raw_unit(g0 + 4 + b) - 3), g0 + b, b, a_hi, a_lo)

            g0 = FIRST["mlp_out"]
            for j in range(16):
                t, n, k0 = j // 4, j % 4 // 2, 16 * (j % 2)
                if j % 4 == 0:
                    e.wait_ge(free["mlp_out"], t + 1)
                if j < 2:
                    e.wait_ge(hid_split, 13 if j == 0 else 16)
                e.wait_ge(raw_used, raw_unit(g0 + j) + 1)
                for k in range(k0, k0 + 16):
                    mm = product(half(t % 2, n), (g0 + j) % SPLIT_SLOTS, k - k0, hid_hi[:, k, :], hid_lo[:, k, :],
                                 k == 0, k == 31)
                    if j == 10 and k - k0 < DT:
                        mod_sum(5, flat(hid[:, :, :]), k - k0)
                mm.then_inc(w_used, 1)
                if j % 4 == 1 and t:
                    sum_squares(SQ["post_ff"] + t - 1, STATN["post_ff"], t == 1, False)
            sum_squares(SQ["post_ff"] + 3, STATN["post_ff"], False, True)
            x_norm("ln1")

            e.wait_ge(const_set, N_CONST)
            g0 = FIRST["z_in"]

            def token_block(j, k0):
                e.wait_ge(raw_used, raw_unit(g0 + j) + 1)
                slot = (g0 + j) % SPLIT_SLOTS
                for c in range(2):
                    dst, tok = ps[:, TOKEN_BANK + c, :], slice(c * P, (c + 1) * P)
                    for k in range(k0, k0 + 4):
                        cols = slice((k - k0) * SG, (k - k0 + 1) * SG)
                        e.matmul(dst, a_hi[:, k, tok], w_hi[:, slot, cols], start=k == 0, stop=False)
                        e.matmul(dst, a_hi[:, k, tok], w_lo[:, slot, cols], start=False, stop=False)
                        mm = e.matmul(dst, a_lo[:, k, tok], w_hi[:, slot, cols], start=False, stop=k == DT - 1)
                mm.then_inc(w_used, 1)

            def scores(p):
                zb = Z_BANKS[p % 2]
                e.wait_ge(qk_ready, 4)
                e.wait_ge(vg_ready, 2)
                if p == 1:
                    e.wait_ge(br_a, 4)
                if p >= 2:
                    e.wait_ge(att_exp, p - 1)
                for h in range(2):
                    f = slice(64 * h, 64 * h + 64)
                    e.matmul(ps[:, zb + h, 0:T], y[f, 4 + p, 0:P], y[f, p, :], start=True, stop=True,
                             skip_group_check=True)
                    mm = e.matmul(ps[:, zb + h, T:T + P], y[f, 4 + p, P:T], y[f, p, P:T], start=False, stop=True,
                                  skip_group_check=True)
                mm.then_inc(z_done, 1)

            def log_weights(p):
                zb = Z_BANKS[p % 2]
                e.wait_ge(sp_masked, p + 1)
                for h in range(2):
                    e.matmul(ps[:, zb + h, 0:T], neg_upper[:, :], sp[:, h, 0:T], start=False, stop=True,
                             skip_group_check=True)
                    e.matmul(ps[:, zb + h, P:T], neg_ones[:, :], sp[:, h, T:T + P], start=False, stop=True,
                             skip_group_check=True)
                    mm = e.matmul(ps[:, zb + h, T:T + P], neg_upper[:, :], sp[:, h, T:T + P], start=False, stop=True,
                                  skip_group_check=True)
                mm.then_inc(loga_done, 1)

            def att_values(p):
                e.wait_ge(att_ready, p + 1)
                if p == 0:
                    e.wait_ge(vv_ready, 2)
                if p:
                    e.wait_ge(br_c, p)
                c0 = T * (p % 2)
                for h in range(2):
                    f = slice(64 * h, 64 * h + 64)
                    cols = slice(64 * (2 * p + h), 64 * (2 * p + h + 1))
                    e.matmul(ps[f, MISC, c0:c0 + T], vv[:, 0, cols], att[:, h, 0:T], start=True, stop=True)
                    mm = e.matmul(ps[f, MISC, c0 + P:c0 + T], vv[:, 1, cols], att[:, h, T:T + P], start=False, stop=True,
                                  skip_group_check=True)
                mm.then_inc(att_done, 1)

            def spatial_gating():
                e.wait_ge(vln_ready, 2)
                e.wait_ge(wm_ready, 2)
                for t in range(4):
                    for c in range(2):
                        for h in range(2):
                            grp = 2 * t + h
                            mm = e.matmul(ps[64 * h:64 * h + 64, SG_BANK + t // 2, T * (t % 2) + c * P:T * (t % 2) + (c + 1) * P],
                                          vg[:, c, 64 * grp:64 * grp + 64], wm[:, grp, :], start=True, stop=True,
                                          skip_group_check=True)
                mm.then_inc(sg_done, 1)

            for s, kind in enumerate(Z_ORDER):
                if kind in ("v", "vv"):
                    first = Z_ORDER[s - 1] != kind
                    if kind == "v" and first:
                        e.wait_ge(vv_ready, 2)
                    token_block(s, 0 if first else 4)
                else:
                    f = Z_FILL[s]
                    if 2 <= f < 6:
                        e.wait_ge(c_in, f - 1)
                    elif 6 <= f < 10:
                        e.wait_ge(qk_raw, f - 5)
                    elif f >= 10:
                        e.wait_ge(z_free_act, f - 9)
                    if s == 0:
                        first_block(act_lo, ACT_TILE["ln1"], raw_unit(g0) + 1, g0, 0, a_hi, a_lo)
                    else:
                        pair_block(raw_unit(g0 + s) + 1, g0 + s, f % 2, a_hi, a_lo)
                if 1 <= s - QK_FIRST <= 4:
                    t = s - QK_FIRST - 1
                    e.wait_ge(sq_ready, SQ["qk"] + t + 1)
                    e.wait_ge(rstd_ready, STATN["qk"] + t)
                    e.matmul(ps[:, STAT, :], head_ones[:, :], sq[:, (SQ["qk"] + t) % 2, :], start=True, stop=True)\
                     .then_inc(sq_used, 1)
                if s == SG_STEP:
                    spatial_gating()
                for p in range(4):
                    if s == AV_STEP(p):
                        att_values(p)
                for p in range(4):
                    if s == U_STEP(p):
                        log_weights(p)
                for p in range(4):
                    if s == QK_STEP(p):
                        scores(p)
                if s == CV_MEAN_STEP:
                    e.wait_ge(conv_step, 4 * CV_TAPS)
                    e.wait_ge(rstd_ready, STATN["cv"])
                    for i in range(4):
                        mm = e.matmul(ps[:, STAT, 0:T], ones[:, :], cacc[:, i, :], start=i == 0, stop=i == 3)
                    mm.then_inc(cv_mean, 1)
                if s == CV_VAR_STEP:
                    e.wait_ge(cv_cent, 4)
                    for t in range(2):
                        sum_squares(SQ["cv"] + t, 0, t == 0, t == 1)

            e.wait_ge(z_free_act, 14)
            g0 = FIRST["branch"]
            with e.Fori(0, N_BLOCKS["branch"] // 4) as it:
                for b in range(4):
                    e.wait_ge(free["branch"], it * 4 + (b + 1))
                    e.wait_ge(raw_used, it * 4 + (raw_unit(g0 + b) + 1))
                    for n, (name, ready) in enumerate((("a", br_a), ("b", br_b), ("c", br_c))):
                        e.wait_ge(ready, 4)
                        for k in range(4):
                            mm = product(half(2 * (b % 2) + n // 2, n % 2), (g0 + b) % SPLIT_SLOTS, 4 * n + k,
                                         br[name][0][:, k, :], br[name][1][:, k, :], k == 0, k == 3)
                    mm.then_inc(w_used, 1)

            g0 = FIRST["mix_out"]
            e.wait_ge(free["branch"], DT - 1 + CREDIT["branch"])
            first_block(mix_ready, 0, raw_unit(g0) + 1, g0, 0, a_hi, a_lo)
            for j in range(1, 4):
                pair_block(raw_unit(g0 + j) + 1, g0 + j, j, a_hi, a_lo)
            x_norm("ln2")

            g0 = FIRST["up"]
            n = N_BLOCKS["up"]
            for b in range(4):
                e.wait_ge(free["up"], b + 1)
                if b == 0:
                    first_block(act_lo, ACT_TILE["ln2"], raw_unit(g0) + 1, g0, 0, a_hi, a_lo)
                else:
                    pair_block(raw_unit(g0 + b) + 1, g0 + b, b, a_hi, a_lo)
            with e.Fori(1, n // 4) as it:
                for b in range(4):
                    e.wait_ge(free["up"], it * 4 + (b + 1))
                    pair_block(it * 4 + (raw_unit(g0 + b) + 1), g0 + b, b, a_hi, a_lo)
            for j in range(n // 4 * 4, n):
                e.wait_ge(free["up"], j + 1)
                pair_block(raw_unit(g0 + j) + 1, g0 + j, j % 4, a_hi, a_lo)

            g0 = FIRST["down"]
            for j in range(16):
                t, n, k0 = j // 4, j % 4 // 2, 11 * (j % 2)
                if j % 4 == 0 and t >= 2:
                    e.wait_ge(out_ready, t - 1)
                if j < 2:
                    e.wait_ge(up_ready, 20 if j == 0 else 22)
                e.wait_ge(raw_used, raw_unit(g0 + j) + 1)
                for k in range(k0, k0 + 11):
                    mm = product(half(2 + t % 2, n), (g0 + j) % SPLIT_SLOTS, k - k0, up_hi[:, k, :], up_lo[:, k, :],
                                 k == 0, k == 21)
                mm.then_inc(w_used, 1)


def _stationary(weight, order, per_block):
    import numpy as np
    k, n = weight.shape
    t = weight.reshape(k // P, P, n // P, P).transpose(2, 0, 1, 3)[np.array(order)]
    return np.ascontiguousarray(t.reshape(-1, per_block, P, P).transpose(0, 2, 1, 3).reshape(-1, P, per_block * P))


def _columns(vector):
    return vector.reshape(-1, P).T


def kernel(**inputs):
    import numpy as np
    import concourse.bacc as bacc
    from concourse.bass_utils import run_bass_kernel_spmd

    a = {name: np.asarray(value) for name, value in inputs.items()}
    per = {name: t for name, _, t in STAGES}
    w = {}
    w["sc_in"] = _stationary(a["sc_w_in"][0], [g + i for i in range(DT) for g in (8, 16, 0)], per["sc_in"])
    w["sc_out"] = _stationary(a["sc_w_out"][0], range(8), per["sc_out"])
    w["mlp_in"] = _stationary(a["mlp_w_in"][0], range(32), per["mlp_in"])
    w["mlp_out"] = _stationary(a["mlp_w_out"][0], range(8), per["mlp_out"])
    w_z = a["w_in_2"][0]

    def token_major(first_col):
        t = w_z[:, first_col:first_col + SG].reshape(2, 4, P, SG)
        return t.transpose(0, 2, 1, 3).reshape(2, P, 4 * SG)

    z_tiles = lambda order: _stationary(w_z, order, per["z_in"])
    w["z_in"] = np.concatenate([
        z_tiles([t + i for i in range(4) for t in (8, 12)]),
        z_tiles(range(16, 24)),
        token_major(3072),
        token_major(512),
        z_tiles(range(0, 4)),
        z_tiles([28 + 8 * br + i for i in range(DT) for br in range(3)]),
    ])
    br = [a[name][0].reshape(4, P, DT, P).transpose(2, 0, 1, 3) for name in ("w_a_out_2", "w_b_out_2", "w_c_out_2")]
    w["branch"] = np.ascontiguousarray(np.stack(br, 1).reshape(DT, 12, P, P).transpose(0, 2, 1, 3).reshape(DT, P, 12 * P))
    w["mix_out"] = _stationary(a["w_out_2"][0], range(8), per["mix_out"])
    gate_value = [t + i for i in range(22) for t in (0, 22)]
    w["up"] = _stationary(a["w_up_2"][0], gate_value, per["up"])
    w["down"] = _stationary(a["w_down_2"][0], range(8), per["down"])

    ada = a["ada_w"][0].reshape(DT, P, 6, D).transpose(2, 0, 1, 3)
    ada_half = ada[[2, 4]].transpose(1, 0, 2, 3).reshape(16, P, D)
    ada = ada[[1, 0, 3, 5]].reshape(16, 2, P, D).transpose(0, 2, 1, 3).reshape(16, P, UNIT)

    taps = lambda t: t.T.reshape(-1, P, t.shape[0]).transpose(1, 0, 2)
    parts = {
        "c": _columns(a["c"][0]), "ada_b": _columns(a["ada_b"][0]), "gains": _columns(a["norm_gains"][0]),
        "sc_conv": taps(a["sc_conv"][0]), "ln1": _columns(a["ln1_g_2"][0]),
        "b_gate": a["b_gate_2"][0].reshape(3, DT, P).transpose(2, 1, 0),
        "cv_w": taps(a["cv_w_2"][0]), "cv_b": _columns(a["cv_b_2"][0]), "cv_g": _columns(a["cv_ln_g_2"][0]),
        "cv_lb": _columns(a["cv_ln_b_2"][0]),
        "qk_g": np.stack([np.tile(a["q_norm_g_2"][0], 2), np.tile(a["k_norm_g_2"][0], 2)], 1),
        "ln2": _columns(a["ln2_g_2"][0]),
        "up_w": taps(a["ffn_conv_w_2"][0])[:, gate_value], "up_b": _columns(a["ffn_conv_b_2"][0])[:, gate_value],
    }
    params = np.concatenate([parts[name].reshape(P, n) for name, n in PARAMS], 1)
    arrays = {
        "x": a["x"][0].T.reshape(DT, P, T).transpose(1, 0, 2), "params": params, "ada": ada, "ada_half": ada_half,
        **{"w_" + name: value for name, value in w.items()},
        "wm_t": a["sg_w_2"][0].transpose(2, 0, 1),
        "sg_bias": np.repeat(a["sg_b_2"][0].reshape(4, 2, 1, P), 64, axis=2).reshape(4, P, P).transpose(1, 0, 2),
        "sg_ln": np.broadcast_to(np.stack([a["sg_ln_g_2"][0], a["sg_ln_b_2"][0]]), (P, 2, SG)),
    }
    arrays = {name: np.ascontiguousarray(value) for name, value in arrays.items()}
    nc = bacc.Bacc("TRN2", target_bir_lowering=False, num_devices=1)
    f32 = mybir.dt.float32
    ap = {name: nc.dram_tensor("in_" + name, value.shape, f32, kind="ExternalInput").ap() for name, value in arrays.items()}
    out = nc.dram_tensor("out", (P, DT, T), f32, kind="ExternalOutput").ap()
    build_program(nc, ap["x"], ap["params"], ap["ada"], ap["ada_half"], {name: ap["w_" + name] for name in w}, ap["wm_t"], ap["sg_bias"],
          ap["sg_ln"], out)
    r = run_bass_kernel_spmd(nc, [{"in_" + name: value for name, value in arrays.items()}], core_ids=[0])
    return r.results[0]["out"].transpose(1, 0, 2).reshape(D, T).T.reshape(1, T, D)
```
